# Optimizing a Trainium2 kernel written in Bass

```python
import jax, jax.numpy as jnp
from jax import lax
import numpy as np

D_MODEL = 4096
BATCH = 1
SEQ = 256
DEPTH = 1

MEM_LEN = 256
HEAD_DIM = 128
DIL_GROUPS = ((128, 1), (512, 4), (2048, 16))
ATTN_WIDTH = 3 * D_MODEL // 8
CONV_WIDTH = 3 * D_MODEL // 8
XATTN_WIDTH = D_MODEL // 4
MIX_WIDTH = ATTN_WIDTH + CONV_WIDTH + XATTN_WIDTH
N_ATTN_HEADS = ATTN_WIDTH // HEAD_DIM
HEADS_PER_DIL = N_ATTN_HEADS // len(DIL_GROUPS)
N_XATTN_HEADS = 4
XATTN_HEAD_DIM = XATTN_WIDTH // N_XATTN_HEADS
CONV_K = 3
IN_COLS = 4 * ATTN_WIDTH + 4 * CONV_WIDTH + 2 * XATTN_WIDTH
BLOCK = 128
ROPE_THETA = 10000.0
EPS = 1e-6
NEG_INF = -1e30

kernel_name = "hybrid_dilated_conv_memory_layer"

def rms_norm(x, g):
    x32 = x.astype(jnp.float32)
    y = x32 * lax.rsqrt(jnp.mean(x32 * x32, axis=-1, keepdims=True) + EPS)
    return (y * g.astype(jnp.float32)).astype(x.dtype)

def rope(x, pos):
    half = x.shape[-1] // 2
    inv = 1.0 / (ROPE_THETA ** (jnp.arange(half, dtype=jnp.float32) / half))
    ang = pos.astype(jnp.float32)[:, None] * inv[None, :]
    cos = jnp.cos(ang)[:, None, :]
    sin = jnp.sin(ang)[:, None, :]
    x32 = x.astype(jnp.float32)
    x1, x2 = x32[..., :half], x32[..., half:]
    return jnp.concatenate([x1 * cos - x2 * sin, x2 * cos + x1 * sin], axis=-1).astype(x.dtype)

def dilated_window_attention(q, k, v, window, dilation):
    b, s, h, dh = q.shape
    steps = window // dilation
    L = s // dilation
    nb = -(-L // BLOCK)
    Lp = nb * BLOCK
    bd = b * dilation

    def to_sub(t):
        t = t.reshape(b, L, dilation, h, dh).transpose(0, 2, 1, 3, 4).reshape(bd, L, h, dh)
        return jnp.pad(t, ((0, 0), (0, Lp - L), (0, 0), (0, 0)))

    def band(t):
        tp = jnp.pad(t, ((0, 0), (BLOCK, 0), (0, 0), (0, 0))).reshape(bd, nb + 1, BLOCK, h, dh)
        return jnp.concatenate([tp[:, :-1], tp[:, 1:]], axis=2)

    qb = to_sub(q).reshape(bd, nb, BLOCK, h, dh)
    kb = band(to_sub(k))
    vb = band(to_sub(v))
    scores = jnp.einsum('znqhd,znkhd->znhqk', qb, kb,
                        preferred_element_type=jnp.float32) * (dh ** -0.5)
    qi = jnp.arange(BLOCK)[:, None]
    kk = jnp.arange(2 * BLOCK)[None, :]
    dist = qi + BLOCK - kk
    key_pos = (jnp.arange(nb)[:, None, None] - 1) * BLOCK + kk[None]
    valid = (dist >= 0) & (dist <= steps) & (key_pos >= 0)
    scores = jnp.where(valid[None, :, None], scores, NEG_INF)
    lse = jax.nn.logsumexp(scores, axis=-1)
    p = jnp.exp(scores - lse[..., None])
    out = jnp.einsum('znhqk,znkhd->znqhd', p.astype(v.dtype), vb)
    out = out.reshape(b, dilation, Lp, h, dh)[:, :, :L].transpose(0, 2, 1, 3, 4).reshape(b, s, h, dh)
    lse = lse.transpose(0, 1, 3, 2).reshape(b, dilation, Lp, h)[:, :, :L]
    lse = lse.transpose(0, 2, 1, 3).reshape(b, s, h)
    return out, lse

def short_conv(u, w):
    s = u.shape[1]
    up = jnp.pad(u, ((0, 0), (CONV_K - 1, 0), (0, 0)))
    y = up[:, 0:s] * w[0]
    for j in range(1, CONV_K):
        y = y + up[:, j:j + s] * w[j]
    return y

def memory_cross_attention(q, mk, mv):
    scores = jnp.einsum('bshd,bmhd->bhsm', q, mk,
                        preferred_element_type=jnp.float32) * (q.shape[-1] ** -0.5)
    p = jax.nn.softmax(scores, axis=-1)
    return jnp.einsum('bhsm,bmhd->bshd', p.astype(mv.dtype), mv)

def setup_inputs(seed: int = 0) -> dict:
    key = jax.random.key(seed)
    ks = jax.random.split(key, 10)
    f32 = jnp.float32
    x = jax.random.normal(ks[0], (BATCH, SEQ, D_MODEL), f32)
    mem = jax.random.normal(ks[1], (BATCH, MEM_LEN, D_MODEL), f32)
    pre_norm = 1.0 + 0.05 * jax.random.normal(ks[2], (DEPTH, D_MODEL), f32)
    w_in = jax.random.normal(ks[3], (DEPTH, D_MODEL, IN_COLS), f32) * D_MODEL ** -0.5
    conv_w = jax.random.normal(ks[4], (DEPTH, CONV_K, CONV_WIDTH), f32) * CONV_K ** -0.5
    mem_norm = 1.0 + 0.05 * jax.random.normal(ks[5], (DEPTH, D_MODEL), f32)
    w_mem_kv = jax.random.normal(ks[6], (DEPTH, D_MODEL, 2 * XATTN_WIDTH), f32) * D_MODEL ** -0.5
    w_out = jax.random.normal(ks[7], (DEPTH, MIX_WIDTH, D_MODEL), f32) * MIX_WIDTH ** -0.5
    post_norm = 1.0 + 0.05 * jax.random.normal(ks[8], (DEPTH, D_MODEL), f32)
    return {"x": x, "mem": mem, "pre_norm": pre_norm, "w_in": w_in, "conv_w": conv_w,
            "mem_norm": mem_norm, "w_mem_kv": w_mem_kv, "w_out": w_out,
            "post_norm": post_norm}

def reference(x, mem, pre_norm, w_in, conv_w, mem_norm, w_mem_kv, w_out, post_norm):
    b, s, _ = x.shape
    m_len = mem.shape[1]
    pos = jnp.arange(s)
    mem_pos = jnp.arange(m_len)
    sizes = (ATTN_WIDTH,) * 4 + (CONV_WIDTH,) * 4 + (XATTN_WIDTH,) * 2
    split_pts = [int(c) for c in np.cumsum(sizes)[:-1]]
    for layer in range(DEPTH):
        h = rms_norm(x, pre_norm[layer])
        proj = h @ w_in[layer]
        q_a, k_a, v_a, z_a, u_c, b_c, c_c, z_c, q_x, z_x = jnp.split(proj, split_pts, axis=-1)

        q_a = rope(q_a.reshape(b, s, N_ATTN_HEADS, HEAD_DIM), pos)
        k_a = rope(k_a.reshape(b, s, N_ATTN_HEADS, HEAD_DIM), pos)
        v_a = v_a.reshape(b, s, N_ATTN_HEADS, HEAD_DIM)
        outs, lses = [], []
        for g, (window, dil) in enumerate(DIL_GROUPS):
            sl = slice(g * HEADS_PER_DIL, (g + 1) * HEADS_PER_DIL)
            o, l = dilated_window_attention(q_a[:, :, sl], k_a[:, :, sl], v_a[:, :, sl], window, dil)
            outs.append(o)
            lses.append(l)
        o = jnp.stack(outs, axis=2)
        alpha = jax.nn.softmax(jnp.stack(lses, axis=2), axis=2)
        y_attn = (o * alpha[..., None].astype(o.dtype)).reshape(b, s, ATTN_WIDTH)
        y_attn = y_attn * jax.nn.silu(z_a)

        y_conv = b_c * short_conv(c_c * u_c, conv_w[layer]) * jax.nn.silu(z_c)

        mkv = rms_norm(mem, mem_norm[layer]) @ w_mem_kv[layer]
        mk, mv = jnp.split(mkv, 2, axis=-1)
        mk = rope(mk.reshape(b, m_len, N_XATTN_HEADS, XATTN_HEAD_DIM), mem_pos)
        mv = mv.reshape(b, m_len, N_XATTN_HEADS, XATTN_HEAD_DIM)
        qx = rope(q_x.reshape(b, s, N_XATTN_HEADS, XATTN_HEAD_DIM), pos + m_len)
        y_x = memory_cross_attention(qx, mk, mv).reshape(b, s, XATTN_WIDTH) * jax.nn.silu(z_x)

        y = jnp.concatenate([y_attn, y_conv, y_x], axis=-1) @ w_out[layer]
        x = x + rms_norm(y, post_norm[layer])
    return x


_drawn_inputs = setup_inputs


def setup_inputs(seed=0):
    import zlib

    import numpy as np

    out = dict(_drawn_inputs(seed))
    spreads = {}
    factors = {'mem_norm': 8.0}
    for name, (base, spread) in spreads.items():
        noise = np.random.default_rng([zlib.crc32(name.encode()), seed]).standard_normal(out[name].shape)
        drawn = base * np.exp(spread * noise) if base else spread * noise
        out[name] = __import__('jax').numpy.asarray(drawn.astype(out[name].dtype))
    for name, factor in factors.items():
        out[name] = (out[name] * factor).astype(out[name].dtype)
    return out
```

```python
import concourse.bass as bass
from concourse import mybir
from contextlib import ExitStack

F32 = mybir.dt.float32
F32R = mybir.dt.float32r
ALU = mybir.AluOpType
ACT = mybir.ActivationFunctionType
AX_X = mybir.AxisListType.X

P = 128
D = 4096
HALVES = 2
TOK = 256
KT = D // P
COLS = 512
RING = 4
CH = 16
MEM_CHUNKS = D // COLS
ATTN_W = CONV_W = 3 * D // 8
X_W = D // 4
HEAD = 128
XHEAD = 256
DILS = 3
HPG = COLS // HEAD
XPG = COLS // XHEAD
KEYS = P + TOK
TAPS = 3
EPS = 1e-6
SCALE = float(HEAD) ** -0.5
XSCALE = float(XHEAD) ** -0.5
LOWEST = -3.0e38

G_MEM, G_X, G_ATTN, G_CONV, G_OUT, G_END = 0, 4, 8, 20, 32, 40
COL_X = 4 * ATTN_W + 4 * CONV_W
OUT_ORDER = [(j + 12) % CH for j in range(CH)]
IN_ORDER = list(range(CH))
Y_CONV, Y_X = ATTN_W // P, (ATTN_W + CONV_W) // P
PE_CUT = 8
EW_CUT = 12
V_PRE, V_MEM, V_CONV = 0, KT, 2 * KT
N_VEC = 2 * KT + TAPS * CONV_W // P


def hybrid_layer(nc, x, mem, pre_norm, w_in, conv_w, mem_norm, w_mem_kv, w_out, post_norm,
                 ident_in, rope_local, rope_q, rope_mem, masks, out):
    x_t = x.rearrange("a (h p) d -> p (a h) d", p=P)
    mem_t = mem.rearrange("a (h p) d -> p (a h) d", p=P)
    out_t = out.rearrange("a (h p) d -> p (a h) d", p=P)
    w_in_t = w_in.rearrange("a (c t p) n -> p (a c) t n", t=2, p=P)
    w_mem_t = w_mem_kv.rearrange("a (c t p) n -> p (a c) t n", t=2, p=P)
    w_out_t = w_out.rearrange("a (c t p) n -> p (a c) t n", t=2, p=P)

    with ExitStack() as ctx:
        KB = 1024
        base = -(-nc.sbuf_base // 64) * 64

        def at(name, kb, shape, dt=F32):
            return nc.alloc_sbuf_tensor_at(name, shape, dt, offset=base + int(kb * KB))

        x_hi = at("x_hi", 0, [P, KT, TOK], F32R)
        x_lo = at("x_lo", 32, [P, KT, TOK], F32R)
        y_norm = at("y_norm", 0, [P, HALVES, D])
        x_res = at("x_res", 32, [P, HALVES, D])
        y_hi = at("y_hi", 64, [P, KT, TOK], F32R)
        y_lo = at("y_lo", 96, [P, KT, TOK], F32R)
        q_t = at("q_t", 64, [P, 4, TOK])
        k_t = at("k_t", 68, [P, 4, TOK])
        v_s = at("v_s", 72, [P, HALVES, COLS])
        probs = at("probs", 76, [P, HPG, KEYS])
        probs_t = at("probs_t", 82, [P, HPG, KEYS])
        xprobs = at("xprobs", 76, [P, XPG, HALVES, TOK])
        xprobs_t = at("xprobs_t", 82, [P, XPG, HALVES, TOK])
        y_x = at("y_x", 96, [P, HALVES, COLS])
        cs_q = at("cs_q", 100, [P, 2, HALVES, XHEAD // 2])
        cs_local = at("cs_local", 102, [P, 2, HALVES, HEAD // 2])
        mask = at("mask", 103, [P, KEYS])
        att_y = at("att_y", 84, [P, HALVES, COLS])
        sig = at("sig", 116, [P, HALVES, COLS])
        raw = at("raw", 128, [P, RING, 2, COLS])
        w_hi = at("w_hi", 144, [P, RING, 2, COLS], F32R)
        w_lo = at("w_lo", 160, [P, RING, 2, COLS], F32R)
        mk_t = at("mk_t", 176, [P, 2 * 4, TOK])
        mv_s = at("mv_s", 184, [P, HALVES, 2, COLS])
        att = at("att", 176, [P, DILS, HALVES, COLS])
        conv_p = at("conv_p", 188, [P, HALVES, COLS])
        x_raw = at("x_raw", 192, [P, HALVES, COLS])
        conv_y = at("conv_y", 192, [P, 4, TOK])
        rot = at("rot", 196, [P, HALVES, COLS])
        b_s = at("b_s", 196, [P, HALVES, COLS])
        rot2 = at("rot2", 200, [P, COLS])
        g_post = at("g_post", 176, [P, D])
        ident = at("ident", 202, [P, P])
        vecs = at("vecs", 202.5, [P, N_VEC])
        cs_mem = at("cs_mem", 203, [P, 2, HALVES, XHEAD // 2])
        vec_rows = at("vec_rows", 205, [N_VEC, P])
        st = at("st", 207, [P, 192])
        squares = at("squares", 205, [P, HALVES, COLS], mybir.dt.bfloat16)
        mem_sq, x_sq, y_sq = (st[:, o:o + 16].rearrange("p (h c) -> p h c", h=2) for o in (0, 16, 32))
        row_sum, row_ms, row_rms = st[:, 48:50], st[:, 50:52], st[:, 52:54]
        mem_rstd, x_rstd, x_nrstd, y_rstd = (st[:, o:o + 2] for o in (54, 56, 58, 60))
        row_max, neg_max, row_exp, row_inv = (st[:, o:o + 8] for o in (64, 72, 80, 88))
        all_neg, all_sum, all_w = (st[:, o:o + 24].rearrange("p (g r) -> p g r", g=DILS)
                                   for o in (96, 120, 144))
        min_neg, den, den2 = (st[:, o:o + 8] for o in (168, 176, 184))

        acc = ctx.enter_context(nc.psum_tensor("acc", [P, 2, HALVES, COLS], F32))
        work = ctx.enter_context(nc.psum_tensor("work", [P, 4, COLS], F32))

        def sem(name):
            return ctx.enter_context(nc.semaphore(name))

        raw_landed = [sem(f"raw_landed{s}") for s in range(RING)]
        slot_seen = sem("slot_seen")
        hi_ready, lo_ready, chunks_used = sem("hi_ready"), sem("lo_ready"), sem("chunks_used")
        acc_free = [sem("acc_free0"), sem("acc_free1")]
        const_landed, mem_tab_landed, tab_landed = sem("const_landed"), sem("mem_tab_landed"), sem("tab_landed")
        mask_landed, post_landed = sem("mask_landed"), sem("post_landed")
        vecs_turned, vecs_ready = sem("vecs_turned"), sem("vecs_ready")
        x_landed, x_turned, x_hi_ready, x_lo_ready = (
            sem("x_landed"), sem("x_turned"), sem("x_hi_ready"), sem("x_lo_ready"))
        rms_step, rstd_ready = sem("rms_step"), sem("rstd_ready")
        rot_step, rot_ready, turned, turned_copied = (
            sem("rot_step"), sem("rot_ready"), sem("turned"), sem("turned_copied"))
        max_ready, sum_kept = sem("max_ready"), sem("sum_kept")
        scored, masked, neg_ready, exp_ready = sem("scored"), sem("masked"), sem("neg_ready"), sem("exp_ready")
        inv_ready = sem("inv_ready")
        probs_turned, probs_copied, mixed = sem("probs_turned"), sem("probs_copied"), sem("mixed")
        z_exp, gate_step, gated = sem("z_exp"), sem("gate_step"), sem("gated")
        fin_turned, fin_hi, fin_lo = sem("fin_turned"), sem("fin_hi"), sem("fin_lo")
        fac_min = sem("fac_min")
        fac_step, fac_exp, fac_ready, att_scaled = (
            sem("fac_step"), sem("fac_exp"), sem("fac_ready"), sem("att_scaled"))
        p_turned, tap2_ready, tap1_ready, conv_ready, y_mul = (
            sem("p_turned"), sem("tap2_ready"), sem("tap1_ready"), sem("conv_ready"), sem("y_mul"))
        sq_ready, y_ready, out_ready, out_landed = (
            sem("sq_ready"), sem("y_ready"), sem("out_ready"), sem("out_landed"))

        def chunk_no(n, j):
            return n * CH + (MEM_CHUNKS + j)

        def group_done(n):
            return n * CH + (MEM_CHUNKS + CH)

        def halves_out(n, par, halves):
            return n + (2 - par + halves)

        block = ctx.enter_context(nc.Block())

        @block.sync
        def _(sp):
            for m in range(MEM_CHUNKS):
                s = m % RING
                if m >= RING:
                    sp.wait_ge(lo_ready, m - RING + 1)
                sp.dma_start(raw[:, s], mem_t[:, :, m * COLS:(m + 1) * COLS]).then_inc(raw_landed[s], 16)

            def load_group(n, weights, col, order):
                for j in range(CH):
                    s = j % RING
                    sp.wait_ge(lo_ready, chunk_no(n, j) - (RING - 1))
                    sp.sem_inc(slot_seen, 1)
                    sp.dma_start(raw[:, s], weights[:, order[j], :, bass.ds(col, COLS)]
                                 ).then_inc(raw_landed[s], 16)

            with sp.Fori(0, 2) as i:
                load_group(i * 2 + G_MEM, w_mem_t, i * COLS, IN_ORDER)
                load_group(i * 2 + (G_MEM + 1), w_mem_t, i * COLS + X_W, IN_ORDER)
            with sp.Fori(0, 2) as i:
                load_group(i * 2 + G_X, w_in_t, i * COLS + COL_X, IN_ORDER)
                load_group(i * 2 + (G_X + 1), w_in_t, i * COLS + (COL_X + X_W), IN_ORDER)
            with sp.Fori(0, DILS) as i:
                for part in range(4):
                    load_group(i * 4 + (G_ATTN + part), w_in_t, i * COLS + part * ATTN_W, IN_ORDER)
            with sp.Fori(0, 3) as i:
                for step, part in enumerate((0, 2, 1, 3)):
                    load_group(i * 4 + (G_CONV + step), w_in_t,
                               i * COLS + (4 * ATTN_W + part * CONV_W), IN_ORDER)
            with sp.Fori(0, 8) as i:
                load_group(i + G_OUT, w_out_t, i * COLS, OUT_ORDER)
            pieces = 0
            for h in range(HALVES):
                for q in range(4):
                    pieces += 1
                    sp.wait_ge(out_ready, pieces)
                    sp.dma_start(out_t[:, h, q * 1024:(q + 1) * 1024],
                                 y_norm[:, h, q * 1024:(q + 1) * 1024]).then_inc(out_landed, 16)
            sp.wait_ge(out_landed, 16 * pieces)

        @block.gpsimd
        def _(pool_q):
            pool_q.dma_start(ident[:], ident_in).then_inc(const_landed, 16)
            pool_q.dma_start(vec_rows[V_PRE:V_PRE + KT, :],
                             pre_norm.rearrange("a (k p) -> (a k) p", p=P)).then_inc(const_landed, 16)
            pool_q.dma_start(vec_rows[V_MEM:V_MEM + KT, :],
                             mem_norm.rearrange("a (k p) -> (a k) p", p=P)).then_inc(const_landed, 16)
            pool_q.dma_start(vec_rows[V_CONV:N_VEC, :],
                             conv_w.rearrange("a t (k p) -> (a t k) p", p=P)).then_inc(const_landed, 16)
            pool_q.dma_start(cs_mem[:], rope_mem).then_inc(mem_tab_landed, 16)
            for m in range(MEM_CHUNKS):
                if m > 0:
                    pool_q.wait_ge(x_lo_ready, m)
                pool_q.dma_start(x_raw[:], x_t[:, :, m * COLS:(m + 1) * COLS]).then_inc(x_landed, 16)
            pool_q.wait_ge(chunks_used, group_done(G_X - 1))
            pool_q.dma_start(cs_q[:], rope_q).then_inc(tab_landed, 16)
            pool_q.dma_start(cs_local[:], rope_local).then_inc(tab_landed, 16)
            pool_q.dma_start(mask[:], masks[0]).then_inc(mask_landed, 16)
            for g in range(1, DILS):
                pool_q.wait_ge(masked, 4 * g)
                pool_q.dma_start(mask[:], masks[g]).then_inc(mask_landed, 16)
            pool_q.wait_ge(chunks_used, group_done(G_OUT - 1))
            pool_q.dma_start(x_res[:], x_t).then_inc(post_landed, 16)
            pool_q.wait_ge(fin_lo, 16)
            pool_q.dma_start(g_post[:], post_norm.partition_broadcast(P)).then_inc(post_landed, 16)

        @block.tensor
        def _(pe):
            def turn_piece(src, banks, done):
                for t in range(4):
                    for h in range(HALVES):
                        last = nc.tensor.transpose(
                            work[:, banks[t // 2], (t % 2) * TOK + h * P:(t % 2) * TOK + (h + 1) * P],
                            src[:, h, t * P:(t + 1) * P], ident[:])
                last.then_inc(done, 1)

            def chunks(n, par, first, last, hi, lo, order=IN_ORDER):
                for j in range(first, last):
                    s = j % RING
                    if j == 0:
                        pe.wait_ge(acc_free[par], halves_out(n, par, 0))
                    if order is OUT_ORDER and j == CH - 2:
                        pe.wait_ge(fin_lo, 16)
                    pe.wait_ge(hi_ready, chunk_no(n, j) + 1)
                    pe.wait_ge(lo_ready, chunk_no(n, j) + 1)
                    for t in range(2):
                        k = 2 * order[j] + t
                        for h in range(HALVES):
                            into, tok = acc[:, par, h], slice(h * P, (h + 1) * P)
                            start, stop = j == 0 and t == 0, j == CH - 1 and t == 1
                            nc.tensor.matmul(into, hi[:, k, tok], w_hi[:, s, t], start=start, stop=False)
                            nc.tensor.matmul(into, hi[:, k, tok], w_lo[:, s, t], start=False, stop=False)
                            mm = nc.tensor.matmul(into, lo[:, k, tok], w_hi[:, s, t], start=False, stop=stop)
                    mm.then_inc(chunks_used, 1)

            def turn_x(m):
                pe.wait_ge(x_landed, m * 16 + 16)
                turn_piece(x_raw, (2, 3), x_turned)

            def turn_rotated(r, banks):
                pe.wait_ge(rot_ready, r * 4 + 4)
                turn_piece(rot, banks, turned)

            def turn_final(src, banks, ready, count):
                pe.wait_ge(ready, count)
                turn_piece(src, banks, fin_turned)

            pe.wait_ge(const_landed, 64)
            nc.tensor.transpose(work[:, 0, 0:N_VEC], vec_rows[:], ident[0:N_VEC, 0:N_VEC]).then_inc(vecs_turned, 1)
            for m in range(MEM_CHUNKS):
                pe.wait_ge(raw_landed[m % RING], 16 * (m // RING + 1))
                if m == 0:
                    pe.wait_ge(vecs_ready, 1)
                if m >= 2:
                    pe.wait_ge(lo_ready, m - 1)
                turn_piece(raw[:, m % RING], (0, 1) if m % 2 == 0 else (2, 3), chunks_used)

            with pe.Fori(0, 2) as i:
                n = i * 2 + G_MEM
                chunks(n, 0, 0, 1, y_hi, y_lo)
                turn_x(i * 4)
                chunks(n, 0, 1, 9, y_hi, y_lo)
                turn_x(i * 4 + 1)
                chunks(n, 0, 9, CH, y_hi, y_lo)
                n = i * 2 + (G_MEM + 1)
                chunks(n, 1, 0, 1, y_hi, y_lo)
                turn_x(i * 4 + 2)
                chunks(n, 1, 1, 4, y_hi, y_lo)
                turn_rotated(i, (0, 1))
                chunks(n, 1, 4, 9, y_hi, y_lo)
                turn_x(i * 4 + 3)
                chunks(n, 1, 9, CH, y_hi, y_lo)

            pe.wait_ge(x_lo_ready, MEM_CHUNKS)
            chunks(G_X, 0, 0, PE_CUT, x_hi, x_lo)
            with pe.Fori(0, 2) as i:
                chunks(i * 2 + G_X, 0, PE_CUT, CH, x_hi, x_lo)
                n = i * 2 + (G_X + 1)
                chunks(n, 1, 0, 4, x_hi, x_lo)
                turn_rotated(i + 2, (0, 1))
                chunks(n, 1, 4, 6, x_hi, x_lo)
                pe.wait_ge(turned_copied, i * 2 + 6)
                for hd in range(XPG):
                    for q in range(HALVES):
                        for d in range(2):
                            mm = nc.tensor.matmul(
                                work[:, 2 + hd, q * TOK:(q + 1) * TOK],
                                q_t[:, 2 * hd + d, q * P:(q + 1) * P],
                                mk_t[:, bass.ds(i * 4 + (2 * hd + d), 1), :].rearrange("p a b -> p (a b)"),
                                start=(d == 0), stop=(d == 1))
                    mm.then_inc(scored, 1)
                chunks(n, 1, 6, 8, x_hi, x_lo)
                for hd in range(XPG):
                    pe.wait_ge(exp_ready, i * 4 + (2 * hd + 2))
                    for kk in range(HALVES):
                        for q in range(HALVES):
                            tr = nc.tensor.transpose(
                                work[:, hd, kk * TOK + q * P:kk * TOK + (q + 1) * P],
                                xprobs[:, hd, q, kk * P:(kk + 1) * P], ident[:])
                    tr.then_inc(probs_turned, 1)
                chunks(n, 1, 8, 10, x_hi, x_lo)
                pe.wait_ge(probs_copied, i * 2 + 2)
                pe.wait_ge(acc_free[1], halves_out(G_X - 1, 1, 2))
                for q in range(HALVES):
                    for hd in range(XPG):
                        for kk in range(HALVES):
                            mm = nc.tensor.matmul(
                                work[:, 2 + q, hd * XHEAD:(hd + 1) * XHEAD],
                                xprobs_t[:, hd, kk, q * P:(q + 1) * P],
                                mv_s[:, kk, bass.ds(i, 1), hd * XHEAD:(hd + 1) * XHEAD]
                                .rearrange("p a b -> p (a b)"),
                                start=(kk == 0), stop=(kk == 1))
                    mm.then_inc(mixed, 1)
                chunks(n, 1, 10, CH, x_hi, x_lo)
                n = i * 2 + (G_X + 2)
                chunks(n, 0, 0, 6, x_hi, x_lo)
                turn_final(y_x, (0, 1), gated, i * 2 + 2)
                chunks(n, 0, 6, PE_CUT, x_hi, x_lo)

            with pe.Fori(0, DILS) as i:
                n = i * 4 + G_ATTN
                chunks(n, 0, PE_CUT, CH, x_hi, x_lo)
                chunks(n + 1, 1, 0, 4, x_hi, x_lo)
                turn_rotated(i * 2 + 4, (0, 1))
                chunks(n + 1, 1, 4, CH, x_hi, x_lo)
                chunks(n + 2, 0, 0, 4, x_hi, x_lo)
                turn_rotated(i * 2 + 5, (2, 3))
                chunks(n + 2, 0, 4, 6, x_hi, x_lo)
                pe.wait_ge(turned_copied, i * 4 + 12)
                for hd in range(HPG):
                    nc.tensor.matmul(work[:, hd, 0:P], q_t[:, hd, 0:P], k_t[:, hd, 0:P],
                                     start=True, stop=True)
                    nc.tensor.matmul(work[:, hd, P:KEYS], q_t[:, hd, P:TOK], k_t[:, hd, :],
                                     start=True, stop=True).then_inc(scored, 1)
                chunks(n + 2, 0, 6, 11, x_hi, x_lo)
                for hd in range(HPG):
                    pe.wait_ge(exp_ready, i * 8 + (2 * hd + 10))
                    nc.tensor.transpose(work[:, hd, 0:P], probs[:, hd, 0:P], ident[:])
                    for kk in range(2):
                        tr = nc.tensor.transpose(work[:, hd, (kk + 1) * P:(kk + 2) * P],
                                                 probs[:, hd, (kk + 1) * P:(kk + 2) * P], ident[:])
                    tr.then_inc(probs_turned, 1)
                chunks(n + 2, 0, 11, CH, x_hi, x_lo)
                chunks(n + 3, 1, 0, 5, x_hi, x_lo)
                pe.wait_ge(probs_copied, i * 4 + 8)
                pe.wait_ge(acc_free[0], halves_out(n + 2, 0, 2))
                for hd in range(HPG):
                    nc.tensor.matmul(work[:, 0, hd * HEAD:(hd + 1) * HEAD], probs_t[:, hd, 0:P],
                                     v_s[:, 0, hd * HEAD:(hd + 1) * HEAD],
                                     start=True, stop=True)
                mm = None
                for hd in range(HPG):
                    for kk in range(2):
                        mm = nc.tensor.matmul(work[:, 1, hd * HEAD:(hd + 1) * HEAD],
                                              probs_t[:, hd, (kk + 1) * P:(kk + 2) * P],
                                              v_s[:, kk, hd * HEAD:(hd + 1) * HEAD],
                                              start=(kk == 0), stop=(kk == 1))
                mm.then_inc(mixed, 1)
                chunks(n + 3, 1, 5, CH, x_hi, x_lo)
                chunks(n + 4, 0, 0, PE_CUT, x_hi, x_lo)

            def convolution(i, hi, lo, order):
                n = i * 4 + G_CONV
                chunks(n, 0, PE_CUT, CH, x_hi, x_lo)
                chunks(n + 1, 1, 0, 6, x_hi, x_lo)
                pe.wait_ge(att_scaled, i * 2 + 2)
                turn_piece(att_y, (0, 1), fin_turned)
                chunks(n + 1, 1, 6, CH, x_hi, x_lo)
                chunks(n + 2, 0, 0, 4, x_hi, x_lo)
                pe.wait_ge(acc_free[1], halves_out(n + 1, 1, 2))
                turn_piece(conv_p, (0, 1), p_turned)
                chunks(n + 2, 0, 4, CH, x_hi, x_lo)
                chunks(n + 3, 1, 0, CH, x_hi, x_lo)
                chunks(n + 4, 0, 0, 6, hi, lo, order)
                turn_final(b_s, (2, 3), gated, i * 2 + 12)
                chunks(n + 4, 0, 6, PE_CUT, hi, lo, order)
            with pe.Fori(0, 2) as i:
                convolution(i, x_hi, x_lo, IN_ORDER)
            convolution(2, y_hi, y_lo, OUT_ORDER)

            with pe.Fori(0, 3) as i:
                n = i * 2 + G_OUT
                chunks(n, 0, PE_CUT, CH, y_hi, y_lo, OUT_ORDER)
                chunks(n + 1, 1, 0, CH, y_hi, y_lo, OUT_ORDER)
                chunks(n + 2, 0, 0, PE_CUT, y_hi, y_lo, OUT_ORDER)
            chunks(G_END - 2, 0, PE_CUT, CH, y_hi, y_lo, OUT_ORDER)
            chunks(G_END - 1, 1, 0, CH, y_hi, y_lo, OUT_ORDER)

        @block.scalar
        def _(act):
            def hi(n, first, last):
                for j in range(first, last):
                    s = j % RING
                    act.wait_ge(raw_landed[s], n * (16 * CH // RING) + 16 * ((MEM_CHUNKS + j) // RING + 1))
                    act.wait_ge(chunks_used, chunk_no(n, j) - (RING - 1))
                    nc.scalar.activation(w_hi[:, s], raw[:, s], ACT.Copy).then_inc(hi_ready, 1)

            def split_piece(m, src, dst_hi, banks, gain, sq, tile, done):
                for h in range(HALVES):
                    nc.scalar.activation(squares[:, h], src[:, h], ACT.Square,
                                         accum_out=sq[:, h, bass.ds(m, 1)])
                for t in range(4):
                    last = nc.scalar.activation(
                        dst_hi[:, bass.ds(tile + t, 1), :].rearrange("p a b -> p (a b)"),
                        work[:, banks[t // 2], (t % 2) * TOK:(t % 2 + 1) * TOK], ACT.Copy,
                        scale=vecs[:, bass.ds(tile + (gain + t), 1)])
                last.then_inc(done, 1)

            def split_x(m):
                act.wait_ge(x_turned, m + 1)
                split_piece(m, x_raw, x_hi, (2, 3), V_PRE, x_sq, m * 4, x_hi_ready)

            def copy_turned(r, banks, dst):
                act.wait_ge(turned, r + 1)
                for b in range(2):
                    nc.scalar.activation(dst[:, 2 * b:2 * b + 2], work[:, banks[b]].rearrange("p (a b) -> p a b", a=2),
                                         ACT.Copy).then_inc(turned_copied, 1)

            def evacuate(n, par, dst, rstd):
                act.wait_ge(chunks_used, group_done(n))
                for h in range(HALVES):
                    nc.scalar.activation(dst[h], acc[:, par, h], ACT.Copy, scale=rstd[:, h:h + 1]
                                         ).then_inc(acc_free[par], 1)

            def z_exps(n, par):
                act.wait_ge(chunks_used, group_done(n))
                for h in range(HALVES):
                    nc.scalar.activation(sig[:, h], acc[:, par, h], ACT.Exp, scale=x_nrstd[:, h:h + 1]
                                         ).then_inc(z_exp, 1)

            def final_hi(f, kt, banks):
                act.wait_ge(fin_turned, f + 1)
                for b in range(2):
                    nc.scalar.activation(y_hi[:, bass.ds(kt + 2 * b, 2), :],
                                         work[:, banks[b]].rearrange("p (a b) -> p a b", a=2),
                                         ACT.Copy).then_inc(fin_hi, 1)

            for par in range(2):
                act.sem_inc(acc_free[par], 2)
            act.wait_ge(vecs_ready, 1)
            for m in range(MEM_CHUNKS):
                act.wait_ge(chunks_used, m + 1)
                if m > 0:
                    act.wait_ge(hi_ready, m)
                split_piece(m, raw[:, m % RING], y_hi, (0, 1) if m % 2 == 0 else (2, 3), V_MEM, mem_sq,
                            4 * m, hi_ready)
            act.wait_ge(rms_step, 2)
            nc.scalar.activation(row_rms, row_ms, ACT.Sqrt).then_inc(rms_step, 1)

            hi(G_MEM, 0, 4)
            act.wait_ge(rstd_ready, 1)
            with act.Fori(0, 2) as i:
                n = i * 2 + G_MEM
                hi(n, 4, 6)
                split_x(i * 4)
                hi(n, 6, 13)
                split_x(i * 4 + 1)
                hi(n, 13, CH)
                hi(n + 1, 0, 6)
                split_x(i * 4 + 2)
                hi(n + 1, 6, 8)
                copy_turned(i, (0, 1), mk_t[:, bass.ds(i * 4, 4), :])
                hi(n + 1, 8, 13)
                split_x(i * 4 + 3)
                hi(n + 1, 13, CH)
                hi(n + 2, 0, 4)
                evacuate(n + 1, 1, [mv_s[:, h, bass.ds(i, 1)].rearrange("p a b -> p (a b)") for h in range(2)],
                         mem_rstd)
            hi(G_X, 4, 5)
            act.wait_ge(rms_step, 5)
            nc.scalar.activation(row_rms, row_ms, ACT.Sqrt).then_inc(rms_step, 1)
            hi(G_X, 5, EW_CUT)
            act.wait_ge(rstd_ready, 3)

            with act.Fori(0, 2) as i:
                n = i * 2 + G_X
                hi(n, EW_CUT, CH)
                hi(n + 1, 0, 8)
                copy_turned(i + 2, (0, 1), q_t)
                hi(n + 1, 8, 10)
                for hd in range(XPG):
                    act.wait_ge(neg_ready, i * 2 + (hd + 1))
                    for q in range(HALVES):
                        r = 2 * q + hd
                        nc.scalar.activation(xprobs[:, hd, q], work[:, 2 + hd, q * TOK:(q + 1) * TOK], ACT.Exp,
                                             bias=neg_max[:, r:r + 1], scale=XSCALE,
                                             accum_out=row_exp[:, r:r + 1]).then_inc(exp_ready, 1)
                hi(n + 1, 10, 12)
                for hd in range(XPG):
                    act.wait_ge(probs_turned, i * 2 + (hd + 1))
                    nc.scalar.activation(xprobs_t[:, hd], work[:, hd].rearrange("p (a b) -> p a b", a=2),
                                         ACT.Copy).then_inc(probs_copied, 1)
                hi(n + 1, 12, CH)
                hi(n + 2, 0, 4)
                z_exps(n + 1, 1)
                hi(n + 2, 4, 9)
                final_hi(i, i * 4 + Y_X, (0, 1))
                hi(n + 2, 9, EW_CUT)

            with act.Fori(0, DILS) as i:
                n = i * 4 + G_ATTN
                hi(n, EW_CUT, CH)
                hi(n + 1, 0, 8)
                copy_turned(i * 2 + 4, (0, 1), q_t)
                hi(n + 1, 8, CH)
                hi(n + 2, 0, 8)
                copy_turned(i * 2 + 5, (2, 3), k_t)
                hi(n + 2, 8, 11)
                act.wait_ge(neg_ready, i + 5)
                for hd in range(HPG):
                    for q in range(HALVES):
                        r, keys = q * HPG + hd, slice(q * P, P + q * TOK)
                        nc.scalar.activation(probs[:, hd, keys], probs[:, hd, keys], ACT.Exp,
                                             bias=neg_max[:, r:r + 1], scale=SCALE,
                                             accum_out=row_exp[:, r:r + 1]).then_inc(exp_ready, 1)
                    if hd == 1:
                        hi(n + 2, 11, 12)
                hi(n + 2, 12, 15)
                for hd in range(HPG):
                    act.wait_ge(probs_turned, i * 4 + (hd + 5))
                    nc.scalar.activation(probs_t[:, hd], work[:, hd, 0:KEYS], ACT.Copy
                                         ).then_inc(probs_copied, 1)
                hi(n + 2, 15, CH)
                hi(n + 3, 0, 4)
                evacuate(n + 2, 0, [v_s[:, h] for h in range(2)], x_rstd)
                hi(n + 3, 4, CH)
                hi(n + 4, 0, 4)
                z_exps(n + 3, 1)
                hi(n + 4, 4, EW_CUT)

            act.wait_ge(fac_step, 4)
            nc.scalar.activation(all_w[:], all_w[:], ACT.Exp).then_inc(fac_exp, 1)

            with act.Fori(0, 3) as i:
                n = i * 4 + G_CONV
                hi(n, EW_CUT, CH)
                hi(n + 1, 0, 4)
                evacuate(n, 0, [conv_p[:, h] for h in range(2)], x_rstd)
                hi(n + 1, 4, 10)
                final_hi(i * 2 + 2, i * 4, (0, 1))
                hi(n + 1, 10, CH)
                hi(n + 2, 0, 8)
                act.wait_ge(p_turned, i + 1)
                for t in range(4):
                    nc.scalar.activation(conv_y[:, t], work[:, t // 2, (t % 2) * TOK:(t % 2 + 1) * TOK], ACT.Copy,
                                         scale=vecs[:, bass.ds(i * 4 + (V_CONV + 2 * (CONV_W // P) + t), 1)]
                                         ).then_inc(tap2_ready, 1)
                hi(n + 2, 8, CH)
                hi(n + 3, 0, 4)
                evacuate(n + 2, 0, [b_s[:, h] for h in range(2)], x_rstd)
                hi(n + 3, 4, CH)
                hi(n + 4, 0, 4)
                z_exps(n + 3, 1)
                hi(n + 4, 4, 10)
                for b in range(2):
                    act.wait_ge(y_mul, i * 2 + (b + 1))
                    nc.scalar.activation(y_hi[:, bass.ds(i * 4 + (Y_CONV + 2 * b), 2), :],
                                         conv_y[:, 2 * b:2 * b + 2], ACT.Copy).then_inc(fin_hi, 1)
                hi(n + 4, 10, EW_CUT)

            def square_rows(n, par, g):
                act.wait_ge(chunks_used, group_done(n))
                for h in range(HALVES):
                    nc.scalar.activation(squares[:, h], acc[:, par, h], ACT.Square,
                                         accum_out=y_sq[:, h, bass.ds(g, 1)]).then_inc(sq_ready, 1)
            with act.Fori(0, 3) as i:
                n = i * 2 + G_OUT
                hi(n, EW_CUT, CH)
                hi(n + 1, 0, 4)
                square_rows(n, 0, i * 2)
                hi(n + 1, 4, CH)
                hi(n + 2, 0, 4)
                square_rows(n + 1, 1, i * 2 + 1)
                hi(n + 2, 4, EW_CUT)
            hi(G_END - 2, EW_CUT, CH)
            hi(G_END - 1, 0, 4)
            square_rows(G_END - 2, 0, 6)
            hi(G_END - 1, 4, CH)
            square_rows(G_END - 1, 1, 7)
            act.wait_ge(rms_step, 8)
            nc.scalar.activation(row_rms, row_ms, ACT.Sqrt).then_inc(rms_step, 1)

        @block.vector
        def _(dve):
            V = nc.vector

            def lo(n, first, last):
                for j in range(first, last):
                    s = j % RING
                    dve.wait_ge(hi_ready, chunk_no(n, j) + 1)
                    V.tensor_tensor(w_lo[:, s], raw[:, s], w_hi[:, s].bitcast(F32), ALU.subtract
                                    ).then_inc(lo_ready, 1)

            def split_piece(dst_hi, dst_lo, banks, gain, tile, done):
                for t in range(4):
                    last = V.scalar_tensor_tensor(
                        dst_lo[:, bass.ds(tile + t, 1), :].rearrange("p a b -> p (a b)"),
                        work[:, banks[t // 2], (t % 2) * TOK:(t % 2 + 1) * TOK],
                        vecs[:, bass.ds(tile + (gain + t), 1)],
                        dst_hi[:, bass.ds(tile + t, 1), :].rearrange("p a b -> p (a b)").bitcast(F32),
                        ALU.mult, ALU.subtract)
                last.then_inc(done, 1)

            def split_x(m):
                dve.wait_ge(x_hi_ready, m + 1)
                split_piece(x_hi, x_lo, (2, 3), V_PRE, m * 4, x_lo_ready)

            def root_mean_square(sq, width, step, rstd, neg=None):
                V.tensor_reduce(row_sum, sq, AX_X, ALU.add).then_inc(rms_step, 1)
                dve.wait_ge(rms_step, step + 1)
                V.tensor_scalar(row_ms, row_sum, 1.0 / width, EPS, ALU.mult, ALU.add).then_inc(rms_step, 1)
                dve.wait_ge(rms_step, step + 3)
                V.reciprocal(rstd, row_rms).then_inc(rstd_ready, 1)

            def rotate(n, par, h, rr, cs, heads, half):
                rstd = (mem_rstd if cs is cs_mem else x_rstd)[:, h:h + 1]
                a = acc[:, par, h].rearrange("p (g s d) -> p g s d", g=heads, s=2)
                o = rot[:, h].rearrange("p (g s d) -> p g s d", g=heads, s=2)
                r2 = rot2[:, :].rearrange("p (s g d) -> p s g d", s=2, g=heads)
                cos = cs[:, 0, h].unsqueeze(1).to_broadcast([P, 2 * heads, half])
                sin = cs[:, 1, h].unsqueeze(1).to_broadcast([P, heads, half])
                dve.wait_ge(chunks_used, group_done(n))
                V.scalar_tensor_tensor(rot[:, h].rearrange("p (g d) -> p g d", d=half),
                                       acc[:, par, h].rearrange("p (g d) -> p g d", d=half),
                                       rstd, cos, ALU.mult, ALU.mult).then_inc(rot_step, 1)
                if h == 1:
                    dve.wait_ge(rot_ready, rr * 2)
                V.scalar_tensor_tensor(r2[:, 0], a[:, :, 1], rstd, sin, ALU.mult, ALU.mult).then_inc(rot_step, 1)
                V.scalar_tensor_tensor(r2[:, 1], a[:, :, 0], rstd, sin, ALU.mult, ALU.mult
                                       ).then_inc(acc_free[par], 1)
                dve.wait_ge(rot_step, rr * 2 + 2)
                V.tensor_tensor(o[:, :, 0], o[:, :, 0], r2[:, 0], ALU.subtract).then_inc(rot_ready, 1)
                dve.wait_ge(acc_free[par], halves_out(n, par, h + 1))
                V.tensor_tensor(o[:, :, 1], o[:, :, 1], r2[:, 1], ALU.add).then_inc(rot_ready, 1)

            def gate_front(zi):
                for h in range(HALVES):
                    dve.wait_ge(z_exp, zi * 2 + (h + 1))
                    V.tensor_scalar(sig[:, h], sig[:, h], 1.0, None, ALU.add).then_inc(gate_step, 1)
                for h in range(HALVES):
                    dve.wait_ge(gate_step, zi * 4 + (h + 1))
                    V.reciprocal(sig[:, h], sig[:, h]).then_inc(gate_step, 1)

            def gate_back(zi, n, par):
                for h in range(HALVES):
                    dve.wait_ge(gate_step, zi * 4 + (h + 3))
                    V.scalar_tensor_tensor(sig[:, h], acc[:, par, h], x_rstd[:, h:h + 1], sig[:, h],
                                           ALU.mult, ALU.mult).then_inc(acc_free[par], 1)

            def final_lo(f, kt, banks):
                for b in range(2):
                    dve.wait_ge(fin_hi, f * 2 + (b + 1))
                    V.tensor_tensor(y_lo[:, bass.ds(kt + 2 * b, 2), :],
                                    work[:, banks[b]].rearrange("p (a b) -> p a b", a=2),
                                    y_hi[:, bass.ds(kt + 2 * b, 2), :].bitcast(F32), ALU.subtract
                                    ).then_inc(fin_lo, 1)

            dve.wait_ge(vecs_turned, 1)
            V.tensor_copy(vecs[:], work[:, 0, 0:N_VEC]).then_inc(vecs_ready, 1)
            dve.wait_ge(vecs_ready, 1)
            for m in range(MEM_CHUNKS):
                dve.wait_ge(hi_ready, m + 1)
                split_piece(y_hi, y_lo, (0, 1) if m % 2 == 0 else (2, 3), V_MEM, 4 * m, lo_ready)
            root_mean_square(mem_sq, D, 0, mem_rstd)
            dve.wait_ge(mem_tab_landed, 16)
            dve.wait_ge(rstd_ready, 1)

            lo(G_MEM, 0, 4)
            with dve.Fori(0, 2) as i:
                n = i * 2 + G_MEM
                lo(n, 4, 6)
                split_x(i * 4)
                lo(n, 6, 13)
                split_x(i * 4 + 1)
                lo(n, 13, CH)
                lo(n + 1, 0, 4)
                rotate(n, 0, 0, i * 2, cs_mem, XPG, XHEAD // 2)
                lo(n + 1, 4, 5)
                rotate(n, 0, 1, i * 2 + 1, cs_mem, XPG, XHEAD // 2)
                lo(n + 1, 5, 6)
                split_x(i * 4 + 2)
                lo(n + 1, 6, 13)
                split_x(i * 4 + 3)
                lo(n + 1, 13, CH)
                lo(n + 2, 0, 4)
            root_mean_square(x_sq, D, 3, x_rstd)
            lo(G_X, 4, 5)
            dve.wait_ge(rstd_ready, 2)
            V.tensor_scalar(x_nrstd, x_rstd, -1.0, None, ALU.mult).then_inc(rstd_ready, 1)
            lo(G_X, 5, EW_CUT)
            dve.wait_ge(tab_landed, 32)

            with dve.Fori(0, 2) as i:
                n = i * 2 + G_X
                lo(n, EW_CUT, CH)
                lo(n + 1, 0, 4)
                rotate(n, 0, 0, i * 2 + 4, cs_q, XPG, XHEAD // 2)
                lo(n + 1, 4, 5)
                rotate(n, 0, 1, i * 2 + 5, cs_q, XPG, XHEAD // 2)
                lo(n + 1, 5, 10)
                for hd in range(XPG):
                    dve.wait_ge(scored, i * 2 + (hd + 1))
                    V.tensor_reduce(row_max[:, 2 * hd:2 * hd + 2],
                                    work[:, 2 + hd].rearrange("p (q k) -> p q k", q=2), AX_X, ALU.max
                                    ).then_inc(max_ready, 1)
                    dve.wait_ge(max_ready, i * 2 + (hd + 1))
                    V.tensor_scalar(neg_max[:, 0:4].rearrange("p (q g) -> p g q", g=2)[:, hd],
                                    row_max[:, 2 * hd:2 * hd + 2], -XSCALE, None, ALU.mult
                                    ).then_inc(neg_ready, 1)
                lo(n + 1, 10, 13)
                dve.wait_ge(exp_ready, i * 4 + 4)
                V.reciprocal(row_inv[:, 0:4], row_exp[:, 0:4]).then_inc(inv_ready, 1)
                lo(n + 1, 13, CH)
                lo(n + 2, 0, 5)
                gate_front(i)
                lo(n + 2, 5, 6)
                gate_back(i, n + 1, 1)
                dve.wait_ge(inv_ready, i + 1)
                for q in range(HALVES):
                    dve.wait_ge(acc_free[1], halves_out(n + 1, 1, q + 1))
                    dve.wait_ge(mixed, i * 2 + (q + 1))
                    for hd in range(XPG):
                        last = V.scalar_tensor_tensor(
                            y_x[:, q, hd * XHEAD:(hd + 1) * XHEAD], work[:, 2 + q, hd * XHEAD:(hd + 1) * XHEAD],
                            row_inv[:, 2 * q + hd:2 * q + hd + 1], sig[:, q, hd * XHEAD:(hd + 1) * XHEAD],
                            ALU.mult, ALU.mult)
                    last.then_inc(gated, 1)
                lo(n + 2, 6, 9)
                final_lo(i, i * 4 + Y_X, (0, 1))
                lo(n + 2, 9, EW_CUT)

            with dve.Fori(0, DILS) as i:
                n = i * 4 + G_ATTN
                lo(n, EW_CUT, CH)
                lo(n + 1, 0, 4)
                rotate(n, 0, 0, i * 4 + 8, cs_local, HPG, HEAD // 2)
                lo(n + 1, 4, 5)
                rotate(n, 0, 1, i * 4 + 9, cs_local, HPG, HEAD // 2)
                lo(n + 1, 5, CH)
                lo(n + 2, 0, 4)
                rotate(n + 1, 1, 0, i * 4 + 10, cs_local, HPG, HEAD // 2)
                lo(n + 2, 4, 5)
                rotate(n + 1, 1, 1, i * 4 + 11, cs_local, HPG, HEAD // 2)
                lo(n + 2, 5, 10)
                dve.wait_ge(mask_landed, i * 16 + 16)
                for hd in range(HPG):
                    dve.wait_ge(scored, i * 4 + (hd + 5))
                    V.tensor_tensor(probs[:, hd], work[:, hd, 0:KEYS], mask[:], ALU.add).then_inc(masked, 1)
                    if hd == 1:
                        lo(n + 2, 10, 11)
                dve.wait_ge(masked, i * 4 + 4)
                for q in range(HALVES):
                    V.tensor_reduce(row_max[:, q * HPG:(q + 1) * HPG], probs[:, :, q * P:P + q * TOK], AX_X, ALU.max
                                    ).then_inc(max_ready, 1)
                dve.wait_ge(max_ready, i * 2 + 6)
                V.tensor_scalar(neg_max[:], row_max[:], -SCALE, None, ALU.mult).then_inc(neg_ready, 1)
                V.tensor_scalar(all_neg[:, bass.ds(i, 1)].rearrange("p a b -> p (a b)"), row_max[:], -SCALE, None,
                                ALU.mult).then_inc(fac_step, 1)
                lo(n + 2, 11, CH)
                lo(n + 3, 0, 2)
                dve.wait_ge(exp_ready, i * 8 + 16)
                V.tensor_copy(all_sum[:, bass.ds(i, 1)].rearrange("p a b -> p (a b)"), row_exp[:]
                              ).then_inc(sum_kept, 1)
                lo(n + 3, 2, CH)
                lo(n + 4, 0, 5)
                gate_front(i + 2)
                lo(n + 4, 5, 6)
                gate_back(i + 2, n + 3, 1)
                for q in range(HALVES):
                    dve.wait_ge(acc_free[1], halves_out(n + 3, 1, q + 1))
                    dve.wait_ge(mixed, i + 5)
                    V.tensor_tensor(att[:, bass.ds(i, 1), q].rearrange("p a b -> p (a b)"), work[:, q], sig[:, q],
                                    ALU.mult).then_inc(gated, 1)
                lo(n + 4, 6, EW_CUT)

            dve.wait_ge(fac_step, DILS)
            dve.wait_ge(sum_kept, DILS)
            V.tensor_tensor(min_neg, all_neg[:, 0], all_neg[:, 1], ALU.min).then_inc(fac_min, 1)
            dve.wait_ge(fac_min, 1)
            V.tensor_tensor(min_neg, min_neg, all_neg[:, 2], ALU.min).then_inc(fac_min, 1)
            dve.wait_ge(fac_min, 2)
            V.tensor_tensor(all_w[:], min_neg.unsqueeze(1).to_broadcast([P, DILS, 8]), all_neg[:], ALU.subtract
                            ).then_inc(fac_step, 1)
            dve.wait_ge(fac_exp, 1)
            V.tensor_tensor(all_sum[:], all_sum[:], all_w[:], ALU.mult).then_inc(fac_min, 1)
            dve.wait_ge(fac_min, 3)
            V.tensor_tensor(den, all_sum[:, 0], all_sum[:, 1], ALU.add).then_inc(fac_min, 1)
            dve.wait_ge(fac_min, 4)
            V.tensor_tensor(den, den, all_sum[:, 2], ALU.add).then_inc(fac_min, 1)
            dve.wait_ge(fac_min, 5)
            V.reciprocal(den2, den).then_inc(fac_min, 1)
            dve.wait_ge(fac_min, 6)
            V.tensor_tensor(all_w[:], all_w[:], den2.unsqueeze(1).to_broadcast([P, DILS, 8]), ALU.mult
                            ).then_inc(fac_ready, 1)
            dve.wait_ge(fac_ready, 1)

            def tap(i, t, k, ready):
                shift = TAPS - 1 - k
                V.scalar_tensor_tensor(conv_y[:, t, shift:TOK],
                                       work[:, t // 2, (t % 2) * TOK:(t % 2 + 1) * TOK - shift],
                                       vecs[:, bass.ds(i * 4 + (V_CONV + k * (CONV_W // P) + t), 1)],
                                       conv_y[:, t, shift:TOK], ALU.mult, ALU.add).then_inc(ready, 1)
            with dve.Fori(0, 3) as i:
                n = i * 4 + G_CONV
                lo(n, EW_CUT, CH)
                lo(n + 1, 0, 6)
                for h in range(HALVES):
                    a = att[:, bass.ds(i, 1), h].rearrange("p a (g d) -> p (a g) d", g=HPG)
                    f = all_w[:, bass.ds(i, 1), h * HPG:(h + 1) * HPG].rearrange("p a g -> p (a g)")
                    V.tensor_tensor(att_y[:, h].rearrange("p (g d) -> p g d", g=HPG), a, f.unsqueeze(2).to_broadcast([P, HPG, HEAD]), ALU.mult
                                    ).then_inc(att_scaled, 1)
                lo(n + 1, 6, 10)
                final_lo(i * 2 + 2, i * 4, (0, 1))
                lo(n + 1, 10, CH)
                lo(n + 2, 0, 4)
                dve.wait_ge(chunks_used, group_done(n + 1))
                dve.wait_ge(acc_free[0], halves_out(n, 0, 2))
                for h in range(HALVES):
                    V.scalar_tensor_tensor(conv_p[:, h], acc[:, 1, h], x_rstd[:, h:h + 1], conv_p[:, h],
                                           ALU.mult, ALU.mult).then_inc(acc_free[1], 1)
                lo(n + 2, 4, 8)
                for b in range(2):
                    dve.wait_ge(tap2_ready, i * 4 + (2 * b + 2))
                    for t in (2 * b, 2 * b + 1):
                        tap(i, t, 1, tap1_ready)
                    for t in (2 * b, 2 * b + 1):
                        dve.wait_ge(tap1_ready, i * 4 + (t + 1))
                        tap(i, t, 0, conv_ready)
                    lo(n + 2, 8 + b, 9 + b)
                lo(n + 2, 10, CH)
                lo(n + 3, 0, CH)
                lo(n + 4, 0, 5)
                gate_front(i + 5)
                lo(n + 4, 5, 6)
                gate_back(i + 5, n + 3, 1)
                dve.wait_ge(acc_free[0], halves_out(n + 2, 0, 2))
                for h in range(HALVES):
                    dve.wait_ge(acc_free[1], halves_out(n + 3, 1, h + 1))
                    V.tensor_tensor(b_s[:, h], b_s[:, h], sig[:, h], ALU.mult).then_inc(gated, 1)
                lo(n + 4, 6, 9)
                dve.wait_ge(fin_turned, i * 2 + 4)
                dve.wait_ge(conv_ready, i * 4 + 4)
                for b in range(2):
                    V.tensor_tensor(conv_y[:, 2 * b:2 * b + 2], conv_y[:, 2 * b:2 * b + 2],
                                    work[:, 2 + b].rearrange("p (a b) -> p a b", a=2), ALU.mult).then_inc(y_mul, 1)
                lo(n + 4, 9, 10)
                for b in range(2):
                    dve.wait_ge(fin_hi, i * 4 + (b + 7))
                    V.tensor_tensor(y_lo[:, bass.ds(i * 4 + (Y_CONV + 2 * b), 2), :], conv_y[:, 2 * b:2 * b + 2],
                                    y_hi[:, bass.ds(i * 4 + (Y_CONV + 2 * b), 2), :].bitcast(F32), ALU.subtract
                                    ).then_inc(fin_lo, 1)
                lo(n + 4, 10, EW_CUT)

            def gain_rows(n, par, g):
                for h in range(HALVES):
                    dve.wait_ge(sq_ready, g * 2 + (h + 1))
                    V.tensor_tensor(y_norm[:, h, bass.ds(g * COLS, COLS)], acc[:, par, h],
                                    g_post[:, bass.ds(g * COLS, COLS)], ALU.mult).then_inc(acc_free[par], 1)
            with dve.Fori(0, 3) as i:
                n = i * 2 + G_OUT
                lo(n, EW_CUT, CH)
                lo(n + 1, 0, 6)
                dve.wait_ge(post_landed, 32)
                gain_rows(n, 0, i * 2)
                lo(n + 1, 6, CH)
                lo(n + 2, 0, 6)
                gain_rows(n + 1, 1, i * 2 + 1)
                lo(n + 2, 6, EW_CUT)
            lo(G_END - 2, EW_CUT, CH)
            lo(G_END - 1, 0, 6)
            gain_rows(G_END - 2, 0, 6)
            lo(G_END - 1, 6, CH)
            gain_rows(G_END - 1, 1, 7)
            dve.wait_ge(sq_ready, 16)
            root_mean_square(y_sq, D, 6, y_rstd)
            dve.wait_ge(rstd_ready, 4)
            dve.wait_ge(acc_free[1], halves_out(G_END - 1, 1, 2))
            for h in range(HALVES):
                for q in range(4):
                    piece = (slice(None), h, slice(q * 1024, (q + 1) * 1024))
                    V.scalar_tensor_tensor(y_norm[piece], y_norm[piece], y_rstd[:, h:h + 1], x_res[piece],
                                           ALU.mult, ALU.add).then_inc(out_ready, 1)


_INS = ['x', 'mem', 'pre_norm', 'w_in', 'conv_w', 'mem_norm', 'w_mem_kv', 'w_out', 'post_norm']


def _rope_table(first, dim):
    import numpy as np
    half = dim // 2
    inv = (np.float32(1.0) / (np.float32(10000.0) ** (np.arange(half, dtype=np.float32) / np.float32(half))))
    ang = (np.arange(first, first + TOK, dtype=np.float32)[:, None] * inv[None, :].astype(np.float32))
    both = np.stack([np.cos(ang), np.sin(ang)]).astype(np.float32)
    return np.ascontiguousarray(both.reshape(2, HALVES, P, half).transpose(2, 0, 1, 3))


def _mask_table():
    import numpy as np
    out = np.empty((DILS, P, KEYS), np.float32)
    for g, (window, dil) in enumerate(((128, 1), (512, 4), (2048, 16))):
        dist = np.arange(TOK)[:, None] - np.arange(TOK)[None, :]
        seen = (dist >= 0) & (dist <= window) & (dist % dil == 0)
        full = np.where(seen, np.float32(0), np.float32(-1e30))
        out[g, :, :P] = full[:P, :P]
        out[g, :, P:] = full[P:]
    return out


def kernel(**inputs):
    import numpy as _np
    import concourse.bacc as _bacc
    from concourse.bass_utils import run_bass_kernel_spmd as _run

    consts = {
        "ident": _np.eye(P, dtype=_np.float32),
        "rope_local": _rope_table(0, HEAD),
        "rope_q": _rope_table(TOK, XHEAD),
        "rope_mem": _rope_table(0, XHEAD),
        "masks": _mask_table(),
    }
    nc = _bacc.Bacc("TRN2", target_bir_lowering=False, num_devices=1)
    arrays, args = {}, []
    for name, a in [(n, inputs[n]) for n in _INS] + list(consts.items()):
        a = _np.ascontiguousarray(a)
        arrays[f"in_{name}_dram"] = a
        args.append(nc.dram_tensor(f"in_{name}_dram", a.shape, mybir.dt.from_np(a.dtype), kind="ExternalInput").ap())
    args.append(nc.dram_tensor("out_0_dram", (1, TOK, D), F32, kind="ExternalOutput").ap())
    hybrid_layer(nc, *args)
    r = _run(nc, [arrays], core_ids=[0])
    return r.results[0]["out_0_dram"]
```

```python
import concourse.bass as bass
from concourse import mybir
from contextlib import ExitStack

F32 = mybir.dt.float32
F32R = mybir.dt.float32r
ALU = mybir.AluOpType
ACT = mybir.ActivationFunctionType
AX_X = mybir.AxisListType.X

P = 128
D = 4096
HALVES = 2
TOK = 256
KT = D // P
COLS = 512
RING = 4
CH = 16
PIECES = D // COLS
ATTN_W = CONV_W = 3 * D // 8
X_W = D // 4
HEAD = 128
XHEAD = 256
DILS = 3
HPG = COLS // HEAD
XPG = COLS // XHEAD
KEYS = P + TOK
TAPS = 3
EPS = 1e-6
SCALE = float(HEAD) ** -0.5
XSCALE = float(XHEAD) ** -0.5
LOWEST = -3.0e38

G_MEM, G_X, G_ATTN, G_CONV, G_OUT, G_END = 0, 4, 8, 20, 32, 40
COL_X = 4 * ATTN_W + 4 * CONV_W
OUT_ORDER = [(j + 12) % CH for j in range(CH)]
IN_ORDER = list(range(CH))
Y_CONV, Y_X = ATTN_W // P, (ATTN_W + CONV_W) // P
PE_CUT = 8
EW_CUT = 12
V_PRE, V_MEM, V_CONV = 0, KT, 2 * KT
N_VEC = 2 * KT + TAPS * CONV_W // P


def hybrid_layer(nc, x, mem, pre_norm, w_in, conv_w, mem_norm, w_mem_kv, w_out, post_norm,
                 ident_in, rope_local, rope_q, rope_mem, masks, out):
    x_t = x.rearrange("a (h p) d -> p (a h) d", p=P)
    mem_t = mem.rearrange("a (h p) d -> p (a h) d", p=P)
    out_t = out.rearrange("a (h p) d -> p (a h) d", p=P)
    w_in_t = w_in.rearrange("a (c t p) n -> p (a c) t n", t=2, p=P)
    w_mem_t = w_mem_kv.rearrange("a (c t p) n -> p (a c) t n", t=2, p=P)
    w_out_t = w_out.rearrange("a (c t p) n -> p (a c) t n", t=2, p=P)

    with ExitStack() as ctx:
        KB = 1024
        base = -(-nc.sbuf_base // 64) * 64

        def at(name, kb, shape, dt=F32):
            return nc.alloc_sbuf_tensor_at(name, shape, dt, offset=base + int(kb * KB))

        x_hi = at("x_hi", 0, [P, KT, TOK], F32R)
        x_lo = at("x_lo", 32, [P, KT, TOK], F32R)
        y_norm = at("y_norm", 0, [P, HALVES, D])
        x_res = at("x_res", 32, [P, HALVES, D])
        y_hi = at("y_hi", 64, [P, KT, TOK], F32R)
        y_lo = at("y_lo", 96, [P, KT, TOK], F32R)
        q_t = at("q_t", 64, [P, 4, TOK])
        k_t = at("k_t", 68, [P, 4, TOK])
        v_s = at("v_s", 72, [P, HALVES, COLS])
        probs = at("probs", 76, [P, HPG, KEYS])
        probs_t = at("probs_t", 82, [P, HPG, KEYS])
        xprobs = at("xprobs", 76, [P, XPG, HALVES, TOK])
        xprobs_t = at("xprobs_t", 82, [P, XPG, HALVES, TOK])
        y_x = at("y_x", 96, [P, HALVES, COLS])
        cs_q = at("cs_q", 100, [P, 2, HALVES, XHEAD // 2])
        cs_local = at("cs_local", 102, [P, 2, HALVES, HEAD // 2])
        mask = at("mask", 103, [P, KEYS])
        att_y = at("att_y", 84, [P, HALVES, COLS])
        sig = at("sig", 116, [P, HALVES, COLS])
        raw = at("raw", 128, [P, RING, 2, COLS])
        w_hi = at("w_hi", 144, [P, RING, 2, COLS], F32R)
        w_lo = at("w_lo", 160, [P, RING, 2, COLS], F32R)
        mk_t = at("mk_t", 176, [P, 2 * 4, TOK])
        mv_s = at("mv_s", 184, [P, HALVES, 2, COLS])
        att = at("att", 176, [P, DILS, HALVES, COLS])
        conv_p = at("conv_p", 188, [P, HALVES, COLS])
        piece = at("piece", 188, [P, 2, HALVES, COLS])
        conv_y = at("conv_y", 192, [P, 4, TOK])
        rot = at("rot", 196, [P, HALVES, COLS])
        b_s = at("b_s", 196, [P, HALVES, COLS])
        rot2 = at("rot2", 200, [P, COLS])
        g_post = at("g_post", 176, [P, D])
        ident = at("ident", 202, [P, P])
        vecs = at("vecs", 202.5, [P, N_VEC])
        cs_mem = at("cs_mem", 203, [P, 2, HALVES, XHEAD // 2])
        vec_rows = at("vec_rows", 205, [N_VEC, P])
        st = at("st", 207, [P, 192])
        squares = at("squares", 205, [P, HALVES, COLS], mybir.dt.bfloat16)
        mem_sq, x_sq, y_sq = (st[:, o:o + 16].rearrange("p (h c) -> p h c", h=2) for o in (0, 16, 32))
        row_sum, row_ms, row_rms = st[:, 48:50], st[:, 50:52], st[:, 52:54]
        mem_rstd, x_rstd, y_rstd = (st[:, o:o + 2] for o in (54, 56, 58))
        ones = st[:, 60:62]
        row_max, neg_max, row_exp, row_inv = (st[:, o:o + 8] for o in (64, 72, 80, 88))
        all_neg, all_sum, all_w = (st[:, o:o + 24].rearrange("p (g r) -> p g r", g=DILS)
                                   for o in (96, 120, 144))
        min_neg, den, den2 = (st[:, o:o + 8] for o in (168, 176, 184))

        acc = ctx.enter_context(nc.psum_tensor("acc", [P, 2, HALVES, COLS], F32))
        work = ctx.enter_context(nc.psum_tensor("work", [P, 4, COLS], F32))

        def sem(name):
            return ctx.enter_context(nc.semaphore(name))

        raw_landed = [sem(f"raw_landed{s}") for s in range(RING)]
        slot_seen = sem("slot_seen")
        hi_ready, lo_ready, chunks_used = sem("hi_ready"), sem("lo_ready"), sem("chunks_used")
        acc_free = [sem("acc_free0"), sem("acc_free1")]
        ones_ready = sem("ones_ready")
        vecs_landed = sem("vecs_landed")
        const_landed, mem_tab_landed, tab_landed = sem("const_landed"), sem("mem_tab_landed"), sem("tab_landed")
        mask_landed, post_landed = sem("mask_landed"), sem("post_landed")
        vecs_turned, vecs_ready = sem("vecs_turned"), sem("vecs_ready")
        first_landed = [sem("first_landed0"), sem("first_landed1")]
        piece_landed = [sem("piece_landed0"), sem("piece_landed1")]
        piece_turned, piece_hi, piece_lo = sem("piece_turned"), sem("piece_hi"), sem("piece_lo")
        rms_step, rstd_ready = sem("rms_step"), sem("rstd_ready")
        rot_step, rot_ready, turned, turned_copied = (
            sem("rot_step"), sem("rot_ready"), sem("turned"), sem("turned_copied"))
        max_ready, sum_kept = sem("max_ready"), sem("sum_kept")
        scored, masked, neg_ready, exp_ready = sem("scored"), sem("masked"), sem("neg_ready"), sem("exp_ready")
        inv_ready = sem("inv_ready")
        probs_turned, probs_copied, mixed = sem("probs_turned"), sem("probs_copied"), sem("mixed")
        sig_ready, gated = sem("sig_ready"), sem("gated")
        fin_turned, fin_hi, fin_lo = sem("fin_turned"), sem("fin_hi"), sem("fin_lo")
        fac_min = sem("fac_min")
        fac_step, fac_exp, fac_ready, att_scaled = (
            sem("fac_step"), sem("fac_exp"), sem("fac_ready"), sem("att_scaled"))
        p_turned, tap2_ready, tap1_ready, conv_ready, y_mul = (
            sem("p_turned"), sem("tap2_ready"), sem("tap1_ready"), sem("conv_ready"), sem("y_mul"))
        tile_done = sem("tile_done")
        sq_ready, y_ready, out_ready, out_landed = (
            sem("sq_ready"), sem("y_ready"), sem("out_ready"), sem("out_landed"))

        def chunk_no(n, j):
            return n * CH + j

        def first_group(n):
            return isinstance(n, int) and n == G_MEM

        def group_done(n):
            return n * CH + CH

        def piece_slot(m):
            return 1 - m % 2 if m < PIECES else 1

        def piece_wait(eng, m):
            if m < 2:
                eng.wait_ge(first_landed[m], 16)
            else:
                loads = m // 2 if m < PIECES else PIECES // 2 + (m - PIECES)
                eng.wait_ge(piece_landed[piece_slot(m)], 16 * loads)

        def piece_source(m):
            source = mem_t if m < PIECES else x_t
            return source[:, :, m % PIECES * COLS:(m % PIECES + 1) * COLS]

        def halves_out(n, par, halves):
            return n + (2 - par + halves)

        block = ctx.enter_context(nc.Block())

        @block.sync
        def _(sp):
            sp.dma_start(ident[:], ident_in).then_inc(const_landed, 16)
            for m in range(2):
                sp.dma_start(piece[:, piece_slot(m)], piece_source(m)).then_inc(first_landed[m], 16)
                sp.dma_start(raw[:, m], w_mem_t[:, m, :, 0:COLS]).then_inc(raw_landed[m], 16)
            for j in range(2, CH):
                if j >= RING:
                    sp.wait_ge(lo_ready, j - (RING - 1))
                sp.dma_start(raw[:, j % RING], w_mem_t[:, j, :, 0:COLS]).then_inc(raw_landed[j % RING], 16)

            def load_group(n, weights, col, order):
                for j in range(CH):
                    s = j % RING
                    sp.wait_ge(lo_ready, chunk_no(n, j) - (RING - 1))
                    sp.sem_inc(slot_seen, 1)
                    sp.dma_start(raw[:, s], weights[:, order[j], :, bass.ds(col, COLS)]
                                 ).then_inc(raw_landed[s], 16)

            for n, col in ((1, X_W), (2, COLS), (3, X_W + COLS)):
                load_group(n, w_mem_t, col, IN_ORDER)
            with sp.Fori(0, 2) as i:
                load_group(i * 2 + G_X, w_in_t, i * COLS + COL_X, IN_ORDER)
                load_group(i * 2 + (G_X + 1), w_in_t, i * COLS + (COL_X + X_W), IN_ORDER)
            with sp.Fori(0, DILS) as i:
                for part in range(4):
                    load_group(i * 4 + (G_ATTN + part), w_in_t, i * COLS + part * ATTN_W, IN_ORDER)
            with sp.Fori(0, 3) as i:
                for step, part in enumerate((0, 2, 1, 3)):
                    load_group(i * 4 + (G_CONV + step), w_in_t,
                               i * COLS + (4 * ATTN_W + part * CONV_W), IN_ORDER)
            with sp.Fori(0, 8) as i:
                load_group(i + G_OUT, w_out_t, i * COLS, OUT_ORDER)
            pieces = 0
            for h in range(HALVES):
                for col in range(0, D, COLS):
                    pieces += 1
                    sp.wait_ge(out_ready, pieces)
                    sp.dma_start(out_t[:, h, col:col + COLS], y_norm[:, h, col:col + COLS]
                                 ).then_inc(out_landed, 16)
            sp.wait_ge(out_landed, 16 * pieces)

        @block.gpsimd
        def _(pool_q):
            pool_q.dma_start(cs_mem[:], rope_mem).then_inc(mem_tab_landed, 16)
            for m in range(2, 2 * PIECES):
                pool_q.wait_ge(piece_lo, m - 1 if m <= PIECES else m)
                s = piece_slot(m)
                pool_q.dma_start(piece[:, s], piece_source(m)).then_inc(piece_landed[s], 16)
            pool_q.wait_ge(chunks_used, group_done(G_X - 1))
            pool_q.dma_start(cs_q[:], rope_q).then_inc(tab_landed, 16)
            pool_q.dma_start(cs_local[:], rope_local).then_inc(tab_landed, 16)
            pool_q.dma_start(mask[:], masks[0]).then_inc(mask_landed, 16)
            for g in range(1, DILS):
                pool_q.wait_ge(masked, 4 * g)
                pool_q.dma_start(mask[:], masks[g]).then_inc(mask_landed, 16)
            pool_q.wait_ge(chunks_used, group_done(G_OUT - 1))
            pool_q.dma_start(x_res[:], x_t).then_inc(post_landed, 16)
            pool_q.wait_ge(fin_lo, 16)
            pool_q.dma_start(g_post[:], post_norm.partition_broadcast(P)).then_inc(post_landed, 16)

        @block.tensor
        def _(pe):
            def turn_piece(src, banks, done):
                for t in range(4):
                    for h in range(HALVES):
                        last = nc.tensor.transpose(
                            work[:, banks[t // 2], (t % 2) * TOK + h * P:(t % 2) * TOK + (h + 1) * P],
                            src[:, h, t * P:(t + 1) * P], ident[:])
                last.then_inc(done, 1)

            def chunks(n, par, first, last, hi, lo, order=IN_ORDER):
                for j in range(first, last):
                    s = j % RING
                    if j == 0:
                        pe.wait_ge(acc_free[par], halves_out(n, par, 0))
                    if order is OUT_ORDER and j == CH - 2:
                        pe.wait_ge(fin_lo, 16)
                    if first_group(n) and j % 2 == 0:
                        pe.wait_ge(piece_lo, j // 2 + 1)
                    product(chunk_no(n, j), s, j, order[j], par, hi, lo)

            def product(c, s, j, rows, par, hi, lo, halves=range(HALVES), used=True):
                pe.wait_ge(hi_ready, c + 1)
                pe.wait_ge(lo_ready, c + 1)
                for t in range(2):
                    k = 2 * rows + t
                    for h in halves:
                        into, tok = acc[:, par, h], slice(h * P, (h + 1) * P)
                        start, stop = j == 0 and t == 0, j == CH - 1 and t == 1
                        nc.tensor.matmul(into, hi[:, k, tok], w_hi[:, s, t], start=start, stop=False)
                        nc.tensor.matmul(into, hi[:, k, tok], w_lo[:, s, t], start=False, stop=False)
                        mm = nc.tensor.matmul(into, lo[:, k, tok], w_hi[:, s, t], start=False, stop=stop)
                if used:
                    mm.then_inc(chunks_used, 1)
                return mm

            def turn_mem(m):
                piece_wait(pe, m)
                if 2 <= m < PIECES:
                    pe.wait_ge(piece_lo, m - 1)
                elif m > PIECES:
                    pe.wait_ge(piece_lo, m)
                turn_piece(piece[:, piece_slot(m)], (0, 1) if m < PIECES and m % 2 == 0 else (2, 3), piece_turned)

            def turn_x(m):
                turn_mem(PIECES + m)

            def turn_rotated(r, banks):
                pe.wait_ge(rot_ready, r * 4 + 4)
                turn_piece(rot, banks, turned)

            def turn_final(src, banks, ready, count):
                pe.wait_ge(ready, count)
                turn_piece(src, banks, fin_turned)

            pe.wait_ge(const_landed, 16)
            turn_mem(0)
            pe.wait_ge(vecs_landed, 48)
            nc.tensor.transpose(work[:, 2, 0:N_VEC], vec_rows[:], ident[0:N_VEC, 0:N_VEC]).then_inc(vecs_turned, 1)
            pe.wait_ge(vecs_ready, 1)
            for m in range(1, PIECES):
                turn_mem(m)
                chunks(0, 0, 2 * m - 2, 2 * m, y_hi, y_lo)
            chunks(0, 0, CH - 2, CH, y_hi, y_lo)

            chunks(1, 1, 0, 1, y_hi, y_lo)
            turn_x(0)
            chunks(1, 1, 1, 4, y_hi, y_lo)
            turn_rotated(0, (0, 1))
            chunks(1, 1, 4, 7, y_hi, y_lo)
            turn_x(1)
            chunks(1, 1, 7, 11, y_hi, y_lo)
            turn_x(2)
            chunks(1, 1, 11, CH, y_hi, y_lo)
            chunks(2, 0, 0, 1, y_hi, y_lo)
            turn_x(3)
            chunks(2, 0, 1, 6, y_hi, y_lo)
            turn_x(4)
            chunks(2, 0, 6, 11, y_hi, y_lo)
            turn_x(5)
            chunks(2, 0, 11, CH, y_hi, y_lo)
            chunks(3, 1, 0, 1, y_hi, y_lo)
            turn_x(6)
            chunks(3, 1, 1, 4, y_hi, y_lo)
            turn_rotated(1, (0, 1))
            chunks(3, 1, 4, 9, y_hi, y_lo)
            turn_x(7)
            chunks(3, 1, 9, CH, y_hi, y_lo)

            pe.wait_ge(piece_lo, 2 * PIECES)
            chunks(G_X, 0, 0, PE_CUT, x_hi, x_lo)
            with pe.Fori(0, 2) as i:
                chunks(i * 2 + G_X, 0, PE_CUT, CH, x_hi, x_lo)
                n = i * 2 + (G_X + 1)
                chunks(n, 1, 0, 4, x_hi, x_lo)
                turn_rotated(i + 2, (0, 1))
                chunks(n, 1, 4, 6, x_hi, x_lo)
                pe.wait_ge(turned_copied, i * 2 + 6)
                for hd in range(XPG):
                    for q in range(HALVES):
                        for d in range(2):
                            mm = nc.tensor.matmul(
                                work[:, 2 + hd, q * TOK:(q + 1) * TOK],
                                q_t[:, 2 * hd + d, q * P:(q + 1) * P],
                                mk_t[:, bass.ds(i * 4 + (2 * hd + d), 1), :].rearrange("p a b -> p (a b)"),
                                start=(d == 0), stop=(d == 1))
                    mm.then_inc(scored, 1)
                chunks(n, 1, 6, 8, x_hi, x_lo)
                for hd in range(XPG):
                    pe.wait_ge(exp_ready, i * 4 + (2 * hd + 2))
                    for kk in range(HALVES):
                        for q in range(HALVES):
                            tr = nc.tensor.transpose(
                                work[:, hd, kk * TOK + q * P:kk * TOK + (q + 1) * P],
                                xprobs[:, hd, q, kk * P:(kk + 1) * P], ident[:])
                    tr.then_inc(probs_turned, 1)
                chunks(n, 1, 8, 10, x_hi, x_lo)
                pe.wait_ge(probs_copied, i * 2 + 2)
                pe.wait_ge(acc_free[1], halves_out(G_X - 1, 1, 2))
                for q in range(HALVES):
                    for hd in range(XPG):
                        for kk in range(HALVES):
                            mm = nc.tensor.matmul(
                                work[:, 2 + q, hd * XHEAD:(hd + 1) * XHEAD],
                                xprobs_t[:, hd, kk, q * P:(q + 1) * P],
                                mv_s[:, kk, bass.ds(i, 1), hd * XHEAD:(hd + 1) * XHEAD]
                                .rearrange("p a b -> p (a b)"),
                                start=(kk == 0), stop=(kk == 1))
                    mm.then_inc(mixed, 1)
                chunks(n, 1, 10, CH, x_hi, x_lo)
                n = i * 2 + (G_X + 2)
                chunks(n, 0, 0, 6, x_hi, x_lo)
                turn_final(y_x, (0, 1), gated, i * 2 + 2)
                chunks(n, 0, 6, PE_CUT, x_hi, x_lo)

            with pe.Fori(0, DILS) as i:
                n = i * 4 + G_ATTN
                chunks(n, 0, PE_CUT, CH, x_hi, x_lo)
                chunks(n + 1, 1, 0, 4, x_hi, x_lo)
                turn_rotated(i * 2 + 4, (0, 1))
                chunks(n + 1, 1, 4, CH, x_hi, x_lo)
                chunks(n + 2, 0, 0, 4, x_hi, x_lo)
                turn_rotated(i * 2 + 5, (2, 3))
                chunks(n + 2, 0, 4, 6, x_hi, x_lo)
                pe.wait_ge(turned_copied, i * 4 + 12)
                for hd in range(HPG):
                    nc.tensor.matmul(work[:, hd, 0:P], q_t[:, hd, 0:P], k_t[:, hd, 0:P],
                                     start=True, stop=True)
                    nc.tensor.matmul(work[:, hd, P:KEYS], q_t[:, hd, P:TOK], k_t[:, hd, :],
                                     start=True, stop=True).then_inc(scored, 1)
                chunks(n + 2, 0, 6, 11, x_hi, x_lo)
                for hd in range(HPG):
                    pe.wait_ge(exp_ready, i * 8 + (2 * hd + 10))
                    nc.tensor.transpose(work[:, hd, 0:P], probs[:, hd, 0:P], ident[:])
                    for kk in range(2):
                        tr = nc.tensor.transpose(work[:, hd, (kk + 1) * P:(kk + 2) * P],
                                                 probs[:, hd, (kk + 1) * P:(kk + 2) * P], ident[:])
                    tr.then_inc(probs_turned, 1)
                chunks(n + 2, 0, 11, CH, x_hi, x_lo)
                chunks(n + 3, 1, 0, 5, x_hi, x_lo)
                pe.wait_ge(probs_copied, i * 4 + 8)
                pe.wait_ge(acc_free[0], halves_out(n + 2, 0, 2))
                for hd in range(HPG):
                    nc.tensor.matmul(work[:, 0, hd * HEAD:(hd + 1) * HEAD], probs_t[:, hd, 0:P],
                                     v_s[:, 0, hd * HEAD:(hd + 1) * HEAD],
                                     start=True, stop=True)
                for hd in range(HPG):
                    for kk in range(2):
                        mm = nc.tensor.matmul(work[:, 1, hd * HEAD:(hd + 1) * HEAD],
                                              probs_t[:, hd, (kk + 1) * P:(kk + 2) * P],
                                              v_s[:, kk, hd * HEAD:(hd + 1) * HEAD],
                                              start=(kk == 0), stop=(kk == 1))
                mm.then_inc(mixed, 1)
                chunks(n + 3, 1, 5, CH, x_hi, x_lo)
                chunks(n + 4, 0, 0, PE_CUT, x_hi, x_lo)

            def convolution(i, hi, lo, order):
                n = i * 4 + G_CONV
                chunks(n, 0, PE_CUT, CH, x_hi, x_lo)
                chunks(n + 1, 1, 0, 6, x_hi, x_lo)
                pe.wait_ge(att_scaled, i * 2 + 2)
                turn_piece(att_y, (0, 1), fin_turned)
                chunks(n + 1, 1, 6, CH, x_hi, x_lo)
                chunks(n + 2, 0, 0, 4, x_hi, x_lo)
                pe.wait_ge(acc_free[1], halves_out(n + 1, 1, 2))
                turn_piece(conv_p, (0, 1), p_turned)
                chunks(n + 2, 0, 4, CH, x_hi, x_lo)
                chunks(n + 3, 1, 0, CH, x_hi, x_lo)
                chunks(n + 4, 0, 0, 6, hi, lo, order)
                turn_final(b_s, (2, 3), gated, i * 2 + 12)
                chunks(n + 4, 0, 6, PE_CUT, hi, lo, order)
            with pe.Fori(0, 2) as i:
                convolution(i, x_hi, x_lo, IN_ORDER)
            convolution(2, y_hi, y_lo, OUT_ORDER)

            with pe.Fori(0, 3) as i:
                n = i * 2 + G_OUT
                chunks(n, 0, PE_CUT, CH, y_hi, y_lo, OUT_ORDER)
                chunks(n + 1, 1, 0, CH, y_hi, y_lo, OUT_ORDER)
                chunks(n + 2, 0, 0, PE_CUT, y_hi, y_lo, OUT_ORDER)
            chunks(G_END - 2, 0, PE_CUT, CH, y_hi, y_lo, OUT_ORDER)
            last = G_END - 1
            chunks(last, 1, 0, CH - RING, y_hi, y_lo, OUT_ORDER)
            for h in range(HALVES):
                for j in range(CH - RING, CH):
                    mm = product(chunk_no(last, j), j % RING, j, OUT_ORDER[j], 1, y_hi, y_lo, halves=[h], used=False)
                mm.then_inc(tile_done, 1)

        @block.scalar
        def _(act):
            def hi(n, first, last):
                for j in range(first, last):
                    s = j % RING
                    act.wait_ge(raw_landed[s], n * (16 * CH // RING) + 16 * (j // RING + 1))
                    if not first_group(n) or j >= RING:
                        act.wait_ge(chunks_used, chunk_no(n, j) - (RING - 1))
                    nc.scalar.activation(w_hi[:, s], raw[:, s], ACT.Copy).then_inc(hi_ready, 1)

            def square_piece(m, src, sq):
                for h in range(HALVES):
                    nc.scalar.activation(squares[:, h], src[:, h], ACT.Square, accum_out=sq[:, h, m:m + 1])

            def split_piece(dst_hi, banks, gain, tile, done):
                for t in range(4):
                    last = nc.scalar.activation(
                        dst_hi[:, bass.ds(tile + t, 1), :].rearrange("p a b -> p (a b)"),
                        work[:, banks[t // 2], (t % 2) * TOK:(t % 2 + 1) * TOK], ACT.Copy,
                        scale=vecs[:, bass.ds(tile + (gain + t), 1)])
                last.then_inc(done, 1)

            def split_mem(m):
                piece_wait(act, m)
                if m > 0:
                    act.wait_ge(piece_hi, m)
                square_piece(m % PIECES, piece[:, piece_slot(m)], mem_sq if m < PIECES else x_sq)
                act.wait_ge(piece_turned, m + 1)
                if m < PIECES:
                    split_piece(y_hi, (0, 1) if m % 2 == 0 else (2, 3), V_MEM, 4 * m, piece_hi)
                else:
                    split_piece(x_hi, (2, 3), V_PRE, 4 * (m - PIECES), piece_hi)

            def split_x(m):
                split_mem(PIECES + m)

            def copy_turned(r, banks, dst):
                act.wait_ge(turned, r + 1)
                for b in range(2):
                    nc.scalar.activation(dst[:, 2 * b:2 * b + 2], work[:, banks[b]].rearrange("p (a b) -> p a b", a=2),
                                         ACT.Copy).then_inc(turned_copied, 1)

            def evacuate(n, par, dst, rstd):
                act.wait_ge(chunks_used, group_done(n))
                for h in range(HALVES):
                    nc.scalar.activation(dst[h], acc[:, par, h], ACT.Copy, scale=rstd[:, h:h + 1]
                                         ).then_inc(acc_free[par], 1)

            def sigmoids(n, par):
                act.wait_ge(chunks_used, group_done(n))
                for h in range(HALVES):
                    nc.scalar.activation(sig[:, h], acc[:, par, h], ACT.Sigmoid, scale=x_rstd[:, h:h + 1]
                                         ).then_inc(sig_ready, 1)

            def final_hi(f, kt, banks):
                act.wait_ge(fin_turned, f + 1)
                for b in range(2):
                    nc.scalar.activation(y_hi[:, bass.ds(kt + 2 * b, 2), :],
                                         work[:, banks[b]].rearrange("p (a b) -> p a b", a=2),
                                         ACT.Copy).then_inc(fin_hi, 1)

            for first, rows in ((V_MEM, mem_norm.rearrange("a (k p) -> (a k) p", p=P)),
                                (V_PRE, pre_norm.rearrange("a (k p) -> (a k) p", p=P)),
                                (V_CONV, conv_w.rearrange("a t (k p) -> (a t k) p", p=P))):
                act.dma_start(vec_rows[first:first + rows.shape[0], :], rows).then_inc(vecs_landed, 16)
            for par in range(2):
                act.sem_inc(acc_free[par], 2)
            act.wait_ge(ones_ready, 1)
            nc.scalar.activation(ones[:, 1:2], ones[:, 0:1], ACT.Copy)
            act.wait_ge(vecs_ready, 1)
            split_mem(0)
            hi(G_MEM, 0, 2)
            for m in range(1, PIECES):
                hi(G_MEM, 2 * m, 2 * m + 1)
                split_mem(m)
                hi(G_MEM, 2 * m + 1, 2 * m + 2)

            hi(1, 0, 1)
            act.wait_ge(rms_step, 2)
            nc.scalar.activation(row_rms, row_ms, ACT.Sqrt).then_inc(rms_step, 1)
            hi(1, 1, 6)
            split_x(0)
            hi(1, 6, 8)
            copy_turned(0, (0, 1), mk_t[:, 0:4])
            hi(1, 8, 11)
            split_x(1)
            hi(1, 11, 15)
            split_x(2)
            hi(1, 15, CH)
            hi(2, 0, 4)
            act.wait_ge(rstd_ready, 1)
            evacuate(1, 1, [mv_s[:, h, 0] for h in range(2)], mem_rstd)
            hi(2, 4, 6)
            split_x(3)
            hi(2, 6, 10)
            split_x(4)
            hi(2, 10, 15)
            split_x(5)
            hi(2, 15, CH)
            hi(3, 0, 6)
            split_x(6)
            hi(3, 6, 8)
            copy_turned(1, (0, 1), mk_t[:, 4:8])
            hi(3, 8, 13)
            split_x(7)
            hi(3, 13, CH)
            hi(G_X, 0, 4)
            evacuate(3, 1, [mv_s[:, h, 1] for h in range(2)], mem_rstd)
            hi(G_X, 4, 5)
            act.wait_ge(rms_step, 5)
            nc.scalar.activation(row_rms, row_ms, ACT.Sqrt).then_inc(rms_step, 1)
            hi(G_X, 5, EW_CUT)
            act.wait_ge(rstd_ready, 2)

            with act.Fori(0, 2) as i:
                n = i * 2 + G_X
                hi(n, EW_CUT, CH)
                hi(n + 1, 0, 8)
                copy_turned(i + 2, (0, 1), q_t)
                hi(n + 1, 8, 10)
                for hd in range(XPG):
                    act.wait_ge(neg_ready, i * 2 + (hd + 1))
                    for q in range(HALVES):
                        r = 2 * q + hd
                        nc.scalar.activation(xprobs[:, hd, q], work[:, 2 + hd, q * TOK:(q + 1) * TOK], ACT.Exp,
                                             bias=neg_max[:, r:r + 1], scale=XSCALE,
                                             accum_out=row_exp[:, r:r + 1]).then_inc(exp_ready, 1)
                hi(n + 1, 10, 12)
                for hd in range(XPG):
                    act.wait_ge(probs_turned, i * 2 + (hd + 1))
                    nc.scalar.activation(xprobs_t[:, hd], work[:, hd].rearrange("p (a b) -> p a b", a=2),
                                         ACT.Copy).then_inc(probs_copied, 1)
                hi(n + 1, 12, CH)
                hi(n + 2, 0, 4)
                sigmoids(n + 1, 1)
                hi(n + 2, 4, 9)
                final_hi(i, i * 4 + Y_X, (0, 1))
                hi(n + 2, 9, EW_CUT)

            with act.Fori(0, DILS) as i:
                n = i * 4 + G_ATTN
                hi(n, EW_CUT, CH)
                hi(n + 1, 0, 8)
                copy_turned(i * 2 + 4, (0, 1), q_t)
                hi(n + 1, 8, CH)
                hi(n + 2, 0, 8)
                copy_turned(i * 2 + 5, (2, 3), k_t)
                hi(n + 2, 8, 11)
                act.wait_ge(neg_ready, i + 5)
                for hd in range(HPG):
                    for q in range(HALVES):
                        r, keys = q * HPG + hd, slice(q * P, P + q * TOK)
                        nc.scalar.activation(probs[:, hd, keys], probs[:, hd, keys], ACT.Exp,
                                             bias=neg_max[:, r:r + 1], scale=SCALE,
                                             accum_out=row_exp[:, r:r + 1]).then_inc(exp_ready, 1)
                    if hd == 1:
                        hi(n + 2, 11, 12)
                hi(n + 2, 12, 15)
                for hd in range(HPG):
                    act.wait_ge(probs_turned, i * 4 + (hd + 5))
                    nc.scalar.activation(probs_t[:, hd], work[:, hd, 0:KEYS], ACT.Copy
                                         ).then_inc(probs_copied, 1)
                hi(n + 2, 15, CH)
                hi(n + 3, 0, 4)
                evacuate(n + 2, 0, [v_s[:, h] for h in range(2)], x_rstd)
                hi(n + 3, 4, CH)
                hi(n + 4, 0, 4)
                sigmoids(n + 3, 1)
                hi(n + 4, 4, EW_CUT)

            act.wait_ge(fac_step, 4)
            nc.scalar.activation(all_w[:], all_w[:], ACT.Exp).then_inc(fac_exp, 1)

            with act.Fori(0, 3) as i:
                n = i * 4 + G_CONV
                hi(n, EW_CUT, CH)
                hi(n + 1, 0, 4)
                evacuate(n, 0, [conv_p[:, h] for h in range(2)], x_rstd)
                hi(n + 1, 4, 10)
                final_hi(i * 2 + 2, i * 4, (0, 1))
                hi(n + 1, 10, CH)
                hi(n + 2, 0, 8)
                act.wait_ge(p_turned, i + 1)
                for t in range(4):
                    nc.scalar.activation(conv_y[:, t], work[:, t // 2, (t % 2) * TOK:(t % 2 + 1) * TOK], ACT.Copy,
                                         scale=vecs[:, bass.ds(i * 4 + (V_CONV + 2 * (CONV_W // P) + t), 1)]
                                         ).then_inc(tap2_ready, 1)
                hi(n + 2, 8, CH)
                hi(n + 3, 0, 4)
                evacuate(n + 2, 0, [b_s[:, h] for h in range(2)], x_rstd)
                hi(n + 3, 4, CH)
                hi(n + 4, 0, 4)
                sigmoids(n + 3, 1)
                hi(n + 4, 4, 10)
                for b in range(2):
                    act.wait_ge(y_mul, i * 2 + (b + 1))
                    nc.scalar.activation(y_hi[:, bass.ds(i * 4 + (Y_CONV + 2 * b), 2), :],
                                         conv_y[:, 2 * b:2 * b + 2], ACT.Copy).then_inc(fin_hi, 1)
                hi(n + 4, 10, EW_CUT)

            def square_rows(n, par, g):
                act.wait_ge(chunks_used, group_done(n))
                for h in range(HALVES):
                    nc.scalar.activation(squares[:, h], acc[:, par, h], ACT.Square,
                                         accum_out=y_sq[:, h, bass.ds(g, 1)]).then_inc(sq_ready, 1)
            with act.Fori(0, 3) as i:
                n = i * 2 + G_OUT
                hi(n, EW_CUT, CH)
                hi(n + 1, 0, 4)
                square_rows(n, 0, i * 2)
                hi(n + 1, 4, CH)
                hi(n + 2, 0, 4)
                square_rows(n + 1, 1, i * 2 + 1)
                hi(n + 2, 4, EW_CUT)
            hi(G_END - 2, EW_CUT, CH)
            hi(G_END - 1, 0, 4)
            square_rows(G_END - 2, 0, 6)
            hi(G_END - 1, 4, CH)
            nc.scalar.activation(row_rms, ones, ACT.Sqrt)
            for h in range(HALVES):
                act.wait_ge(tile_done, h + 1)
                nc.scalar.activation(squares[:, h], acc[:, 1, h], ACT.Square,
                                     accum_out=y_sq[:, h, 7:8]).then_inc(sq_ready, 1)
                act.wait_ge(rms_step, 8 + 3 * h)
                nc.scalar.activation(row_rms[:, h:h + 1], row_ms[:, h:h + 1], ACT.Sqrt).then_inc(rms_step, 1)

        @block.vector
        def _(dve):
            V = nc.vector

            def lo(n, first, last):
                for j in range(first, last):
                    s = j % RING
                    dve.wait_ge(hi_ready, chunk_no(n, j) + 1)
                    V.tensor_tensor(w_lo[:, s], raw[:, s], w_hi[:, s].bitcast(F32), ALU.subtract
                                    ).then_inc(lo_ready, 1)

            def split_piece(dst_hi, dst_lo, banks, gain, tile, done):
                for t in range(4):
                    last = V.scalar_tensor_tensor(
                        dst_lo[:, bass.ds(tile + t, 1), :].rearrange("p a b -> p (a b)"),
                        work[:, banks[t // 2], (t % 2) * TOK:(t % 2 + 1) * TOK],
                        vecs[:, bass.ds(tile + (gain + t), 1)],
                        dst_hi[:, bass.ds(tile + t, 1), :].rearrange("p a b -> p (a b)").bitcast(F32),
                        ALU.mult, ALU.subtract)
                last.then_inc(done, 1)

            def split_mem(m):
                dve.wait_ge(piece_hi, m + 1)
                if m < PIECES:
                    split_piece(y_hi, y_lo, (0, 1) if m % 2 == 0 else (2, 3), V_MEM, 4 * m, piece_lo)
                else:
                    split_piece(x_hi, x_lo, (2, 3), V_PRE, 4 * (m - PIECES), piece_lo)

            def split_x(m):
                split_mem(PIECES + m)

            def mean_square(sq, step, halves=slice(0, HALVES)):
                V.tensor_reduce(row_sum[:, halves], sq[:, halves], AX_X, ALU.add).then_inc(rms_step, 1)
                dve.wait_ge(rms_step, step + 1)
                V.tensor_scalar(row_ms[:, halves], row_sum[:, halves], 1.0 / D, EPS, ALU.mult, ALU.add
                                ).then_inc(rms_step, 1)

            def rstd_of(rstd, step, halves=slice(0, HALVES)):
                dve.wait_ge(rms_step, step + 3)
                V.reciprocal(rstd[:, halves], row_rms[:, halves]).then_inc(rstd_ready, 1)

            def rotate(n, par, h, rr, cs, heads, half):
                rstd = (mem_rstd if cs is cs_mem else x_rstd)[:, h:h + 1]
                a = acc[:, par, h].rearrange("p (g s d) -> p g s d", g=heads, s=2)
                o = rot[:, h].rearrange("p (g s d) -> p g s d", g=heads, s=2)
                r2 = rot2[:, :].rearrange("p (s g d) -> p s g d", s=2, g=heads)
                cos = cs[:, 0, h].unsqueeze(1).to_broadcast([P, 2 * heads, half])
                sin = cs[:, 1, h].unsqueeze(1).to_broadcast([P, heads, half])
                dve.wait_ge(chunks_used, group_done(n))
                V.scalar_tensor_tensor(rot[:, h].rearrange("p (g d) -> p g d", d=half),
                                       acc[:, par, h].rearrange("p (g d) -> p g d", d=half),
                                       rstd, cos, ALU.mult, ALU.mult).then_inc(rot_step, 1)
                if h == 1:
                    dve.wait_ge(rot_ready, rr * 2)
                V.scalar_tensor_tensor(r2[:, 0], a[:, :, 1], rstd, sin, ALU.mult, ALU.mult).then_inc(rot_step, 1)
                V.scalar_tensor_tensor(r2[:, 1], a[:, :, 0], rstd, sin, ALU.mult, ALU.mult
                                       ).then_inc(acc_free[par], 1)
                dve.wait_ge(rot_step, rr * 2 + 2)
                V.tensor_tensor(o[:, :, 0], o[:, :, 0], r2[:, 0], ALU.subtract).then_inc(rot_ready, 1)
                dve.wait_ge(acc_free[par], halves_out(n, par, h + 1))
                V.tensor_tensor(o[:, :, 1], o[:, :, 1], r2[:, 1], ALU.add).then_inc(rot_ready, 1)

            def gate(zi, n, par):
                for h in range(HALVES):
                    dve.wait_ge(sig_ready, zi * 2 + (h + 1))
                    V.scalar_tensor_tensor(sig[:, h], acc[:, par, h], x_rstd[:, h:h + 1], sig[:, h],
                                           ALU.mult, ALU.mult).then_inc(acc_free[par], 1)

            def final_lo(f, kt, banks):
                for b in range(2):
                    dve.wait_ge(fin_hi, f * 2 + (b + 1))
                    V.tensor_tensor(y_lo[:, bass.ds(kt + 2 * b, 2), :],
                                    work[:, banks[b]].rearrange("p (a b) -> p a b", a=2),
                                    y_hi[:, bass.ds(kt + 2 * b, 2), :].bitcast(F32), ALU.subtract
                                    ).then_inc(fin_lo, 1)

            V.memset(ones[:], 1.0).then_inc(ones_ready, 1)
            dve.wait_ge(vecs_turned, 1)
            V.tensor_copy(vecs[:], work[:, 2, 0:N_VEC]).then_inc(vecs_ready, 1)
            dve.wait_ge(vecs_ready, 1)
            split_mem(0)
            lo(G_MEM, 0, 2)
            for m in range(1, PIECES):
                lo(G_MEM, 2 * m, 2 * m + 1)
                split_mem(m)
                lo(G_MEM, 2 * m + 1, 2 * m + 2)

            mean_square(mem_sq, 0)
            lo(1, 0, 3)
            rstd_of(mem_rstd, 0)
            lo(1, 3, 4)
            dve.wait_ge(mem_tab_landed, 16)
            dve.wait_ge(rstd_ready, 1)
            rotate(0, 0, 0, 0, cs_mem, XPG, XHEAD // 2)
            lo(1, 4, 5)
            rotate(0, 0, 1, 1, cs_mem, XPG, XHEAD // 2)
            lo(1, 5, 6)
            split_x(0)
            lo(1, 6, 11)
            split_x(1)
            lo(1, 11, 15)
            split_x(2)
            lo(1, 15, CH)
            lo(2, 0, 6)
            split_x(3)
            lo(2, 6, 10)
            split_x(4)
            lo(2, 10, 15)
            split_x(5)
            lo(2, 15, CH)
            lo(3, 0, 4)
            rotate(2, 0, 0, 2, cs_mem, XPG, XHEAD // 2)
            lo(3, 4, 5)
            rotate(2, 0, 1, 3, cs_mem, XPG, XHEAD // 2)
            lo(3, 5, 6)
            split_x(6)
            lo(3, 6, 13)
            split_x(7)
            lo(3, 13, CH)
            lo(G_X, 0, 4)
            mean_square(x_sq, 3)
            lo(G_X, 4, 6)
            rstd_of(x_rstd, 3)
            dve.wait_ge(rstd_ready, 2)
            lo(G_X, 6, EW_CUT)
            dve.wait_ge(tab_landed, 32)

            with dve.Fori(0, 2) as i:
                n = i * 2 + G_X
                lo(n, EW_CUT, CH)
                lo(n + 1, 0, 4)
                rotate(n, 0, 0, i * 2 + 4, cs_q, XPG, XHEAD // 2)
                lo(n + 1, 4, 5)
                rotate(n, 0, 1, i * 2 + 5, cs_q, XPG, XHEAD // 2)
                lo(n + 1, 5, 10)
                for hd in range(XPG):
                    dve.wait_ge(scored, i * 2 + (hd + 1))
                    V.tensor_reduce(row_max[:, 2 * hd:2 * hd + 2],
                                    work[:, 2 + hd].rearrange("p (q k) -> p q k", q=2), AX_X, ALU.max
                                    ).then_inc(max_ready, 1)
                    dve.wait_ge(max_ready, i * 2 + (hd + 1))
                    V.tensor_scalar(neg_max[:, 0:4].rearrange("p (q g) -> p g q", g=2)[:, hd],
                                    row_max[:, 2 * hd:2 * hd + 2], -XSCALE, None, ALU.mult
                                    ).then_inc(neg_ready, 1)
                lo(n + 1, 10, 13)
                dve.wait_ge(exp_ready, i * 4 + 4)
                V.reciprocal(row_inv[:, 0:4], row_exp[:, 0:4]).then_inc(inv_ready, 1)
                lo(n + 1, 13, CH)
                lo(n + 2, 0, 5)
                gate(i, n + 1, 1)
                lo(n + 2, 5, 6)
                dve.wait_ge(inv_ready, i + 1)
                for q in range(HALVES):
                    dve.wait_ge(acc_free[1], halves_out(n + 1, 1, q + 1))
                    dve.wait_ge(mixed, i * 2 + (q + 1))
                    for hd in range(XPG):
                        last = V.scalar_tensor_tensor(
                            y_x[:, q, hd * XHEAD:(hd + 1) * XHEAD], work[:, 2 + q, hd * XHEAD:(hd + 1) * XHEAD],
                            row_inv[:, 2 * q + hd:2 * q + hd + 1], sig[:, q, hd * XHEAD:(hd + 1) * XHEAD],
                            ALU.mult, ALU.mult)
                    last.then_inc(gated, 1)
                lo(n + 2, 6, 9)
                final_lo(i, i * 4 + Y_X, (0, 1))
                lo(n + 2, 9, EW_CUT)

            with dve.Fori(0, DILS) as i:
                n = i * 4 + G_ATTN
                lo(n, EW_CUT, CH)
                lo(n + 1, 0, 4)
                rotate(n, 0, 0, i * 4 + 8, cs_local, HPG, HEAD // 2)
                lo(n + 1, 4, 5)
                rotate(n, 0, 1, i * 4 + 9, cs_local, HPG, HEAD // 2)
                lo(n + 1, 5, CH)
                lo(n + 2, 0, 4)
                rotate(n + 1, 1, 0, i * 4 + 10, cs_local, HPG, HEAD // 2)
                lo(n + 2, 4, 5)
                rotate(n + 1, 1, 1, i * 4 + 11, cs_local, HPG, HEAD // 2)
                lo(n + 2, 5, 10)
                dve.wait_ge(mask_landed, i * 16 + 16)
                for hd in range(HPG):
                    dve.wait_ge(scored, i * 4 + (hd + 5))
                    V.tensor_tensor(probs[:, hd], work[:, hd, 0:KEYS], mask[:], ALU.add).then_inc(masked, 1)
                    if hd == 1:
                        lo(n + 2, 10, 11)
                dve.wait_ge(masked, i * 4 + 4)
                for q in range(HALVES):
                    V.tensor_reduce(row_max[:, q * HPG:(q + 1) * HPG], probs[:, :, q * P:P + q * TOK], AX_X, ALU.max
                                    ).then_inc(max_ready, 1)
                dve.wait_ge(max_ready, i * 2 + 6)
                V.tensor_scalar(neg_max[:], row_max[:], -SCALE, None, ALU.mult).then_inc(neg_ready, 1)
                V.tensor_scalar(all_neg[:, bass.ds(i, 1)].rearrange("p a b -> p (a b)"), row_max[:], -SCALE, None,
                                ALU.mult).then_inc(fac_step, 1)
                lo(n + 2, 11, CH)
                lo(n + 3, 0, 2)
                dve.wait_ge(exp_ready, i * 8 + 16)
                V.tensor_copy(all_sum[:, bass.ds(i, 1)].rearrange("p a b -> p (a b)"), row_exp[:]
                              ).then_inc(sum_kept, 1)
                lo(n + 3, 2, CH)
                lo(n + 4, 0, 5)
                gate(i + 2, n + 3, 1)
                lo(n + 4, 5, 6)
                for q in range(HALVES):
                    dve.wait_ge(acc_free[1], halves_out(n + 3, 1, q + 1))
                    dve.wait_ge(mixed, i + 5)
                    V.tensor_tensor(att[:, bass.ds(i, 1), q].rearrange("p a b -> p (a b)"), work[:, q], sig[:, q],
                                    ALU.mult).then_inc(gated, 1)
                lo(n + 4, 6, EW_CUT)

            dve.wait_ge(fac_step, DILS)
            dve.wait_ge(sum_kept, DILS)
            V.tensor_tensor(min_neg, all_neg[:, 0], all_neg[:, 1], ALU.min).then_inc(fac_min, 1)
            dve.wait_ge(fac_min, 1)
            V.tensor_tensor(min_neg, min_neg, all_neg[:, 2], ALU.min).then_inc(fac_min, 1)
            dve.wait_ge(fac_min, 2)
            V.tensor_tensor(all_w[:], min_neg.unsqueeze(1).to_broadcast([P, DILS, 8]), all_neg[:], ALU.subtract
                            ).then_inc(fac_step, 1)
            dve.wait_ge(fac_exp, 1)
            V.tensor_tensor(all_sum[:], all_sum[:], all_w[:], ALU.mult).then_inc(fac_min, 1)
            dve.wait_ge(fac_min, 3)
            V.tensor_tensor(den, all_sum[:, 0], all_sum[:, 1], ALU.add).then_inc(fac_min, 1)
            dve.wait_ge(fac_min, 4)
            V.tensor_tensor(den, den, all_sum[:, 2], ALU.add).then_inc(fac_min, 1)
            dve.wait_ge(fac_min, 5)
            V.reciprocal(den2, den).then_inc(fac_min, 1)
            dve.wait_ge(fac_min, 6)
            V.tensor_tensor(all_w[:], all_w[:], den2.unsqueeze(1).to_broadcast([P, DILS, 8]), ALU.mult
                            ).then_inc(fac_ready, 1)
            dve.wait_ge(fac_ready, 1)

            def tap(i, t, k, ready):
                shift = TAPS - 1 - k
                V.scalar_tensor_tensor(conv_y[:, t, shift:TOK],
                                       work[:, t // 2, (t % 2) * TOK:(t % 2 + 1) * TOK - shift],
                                       vecs[:, bass.ds(i * 4 + (V_CONV + k * (CONV_W // P) + t), 1)],
                                       conv_y[:, t, shift:TOK], ALU.mult, ALU.add).then_inc(ready, 1)
            with dve.Fori(0, 3) as i:
                n = i * 4 + G_CONV
                lo(n, EW_CUT, CH)
                lo(n + 1, 0, 6)
                for h in range(HALVES):
                    a = att[:, bass.ds(i, 1), h].rearrange("p a (g d) -> p (a g) d", g=HPG)
                    f = all_w[:, bass.ds(i, 1), h * HPG:(h + 1) * HPG].rearrange("p a g -> p (a g)")
                    V.tensor_tensor(att_y[:, h].rearrange("p (g d) -> p g d", g=HPG), a, f.unsqueeze(2).to_broadcast([P, HPG, HEAD]), ALU.mult
                                    ).then_inc(att_scaled, 1)
                lo(n + 1, 6, 10)
                final_lo(i * 2 + 2, i * 4, (0, 1))
                lo(n + 1, 10, CH)
                lo(n + 2, 0, 4)
                dve.wait_ge(chunks_used, group_done(n + 1))
                dve.wait_ge(acc_free[0], halves_out(n, 0, 2))
                for h in range(HALVES):
                    V.scalar_tensor_tensor(conv_p[:, h], acc[:, 1, h], x_rstd[:, h:h + 1], conv_p[:, h],
                                           ALU.mult, ALU.mult).then_inc(acc_free[1], 1)
                lo(n + 2, 4, 8)
                for b in range(2):
                    dve.wait_ge(tap2_ready, i * 4 + (2 * b + 2))
                    for t in (2 * b, 2 * b + 1):
                        tap(i, t, 1, tap1_ready)
                    for t in (2 * b, 2 * b + 1):
                        dve.wait_ge(tap1_ready, i * 4 + (t + 1))
                        tap(i, t, 0, conv_ready)
                    lo(n + 2, 8 + b, 9 + b)
                lo(n + 2, 10, CH)
                lo(n + 3, 0, CH)
                lo(n + 4, 0, 5)
                gate(i + 5, n + 3, 1)
                lo(n + 4, 5, 6)
                dve.wait_ge(acc_free[0], halves_out(n + 2, 0, 2))
                for h in range(HALVES):
                    dve.wait_ge(acc_free[1], halves_out(n + 3, 1, h + 1))
                    V.tensor_tensor(b_s[:, h], b_s[:, h], sig[:, h], ALU.mult).then_inc(gated, 1)
                lo(n + 4, 6, 9)
                dve.wait_ge(fin_turned, i * 2 + 4)
                dve.wait_ge(conv_ready, i * 4 + 4)
                for b in range(2):
                    V.tensor_tensor(conv_y[:, 2 * b:2 * b + 2], conv_y[:, 2 * b:2 * b + 2],
                                    work[:, 2 + b].rearrange("p (a b) -> p a b", a=2), ALU.mult).then_inc(y_mul, 1)
                lo(n + 4, 9, 10)
                for b in range(2):
                    dve.wait_ge(fin_hi, i * 4 + (b + 7))
                    V.tensor_tensor(y_lo[:, bass.ds(i * 4 + (Y_CONV + 2 * b), 2), :], conv_y[:, 2 * b:2 * b + 2],
                                    y_hi[:, bass.ds(i * 4 + (Y_CONV + 2 * b), 2), :].bitcast(F32), ALU.subtract
                                    ).then_inc(fin_lo, 1)
                lo(n + 4, 10, EW_CUT)

            def gain_rows(n, par, g):
                for h in range(HALVES):
                    dve.wait_ge(sq_ready, g * 2 + (h + 1))
                    V.tensor_tensor(y_norm[:, h, bass.ds(g * COLS, COLS)], acc[:, par, h],
                                    g_post[:, bass.ds(g * COLS, COLS)], ALU.mult).then_inc(acc_free[par], 1)
            with dve.Fori(0, 3) as i:
                n = i * 2 + G_OUT
                lo(n, EW_CUT, CH)
                lo(n + 1, 0, 6)
                dve.wait_ge(post_landed, 32)
                gain_rows(n, 0, i * 2)
                lo(n + 1, 6, CH)
                lo(n + 2, 0, 6)
                gain_rows(n + 1, 1, i * 2 + 1)
                lo(n + 2, 6, EW_CUT)
            lo(G_END - 2, EW_CUT, CH)
            lo(G_END - 1, 0, 6)
            gain_rows(G_END - 2, 0, 6)
            lo(G_END - 1, 6, CH)
            for h in range(HALVES):
                dve.wait_ge(sq_ready, 15 + h)
                mean_square(y_sq, 6 + 3 * h, slice(h, h + 1))
                V.tensor_tensor(y_norm[:, h, D - COLS:D], acc[:, 1, h], g_post[:, D - COLS:D], ALU.mult
                                ).then_inc(acc_free[1], 1)
                rstd_of(y_rstd, 6 + 3 * h, slice(h, h + 1))
                dve.wait_ge(acc_free[1], halves_out(G_END - 1, 1, h + 1))
                dve.wait_ge(rstd_ready, 3 + h)
                for col in range(0, D, COLS):
                    part = (slice(None), h, slice(col, col + COLS))
                    V.scalar_tensor_tensor(y_norm[part], y_norm[part], y_rstd[:, h:h + 1], x_res[part],
                                           ALU.mult, ALU.add).then_inc(out_ready, 1)


_INS = ['x', 'mem', 'pre_norm', 'w_in', 'conv_w', 'mem_norm', 'w_mem_kv', 'w_out', 'post_norm']


def _rope_table(first, dim):
    import numpy as np
    half = dim // 2
    inv = (np.float32(1.0) / (np.float32(10000.0) ** (np.arange(half, dtype=np.float32) / np.float32(half))))
    ang = (np.arange(first, first + TOK, dtype=np.float32)[:, None] * inv[None, :].astype(np.float32))
    both = np.stack([np.cos(ang), np.sin(ang)]).astype(np.float32)
    return np.ascontiguousarray(both.reshape(2, HALVES, P, half).transpose(2, 0, 1, 3))


def _mask_table():
    import numpy as np
    out = np.empty((DILS, P, KEYS), np.float32)
    for g, (window, dil) in enumerate(((128, 1), (512, 4), (2048, 16))):
        dist = np.arange(TOK)[:, None] - np.arange(TOK)[None, :]
        seen = (dist >= 0) & (dist <= window) & (dist % dil == 0)
        full = np.where(seen, np.float32(0), np.float32(-1e30))
        out[g, :, :P] = full[:P, :P]
        out[g, :, P:] = full[P:]
    return out


def kernel(**inputs):
    import numpy as _np
    import concourse.bacc as _bacc
    from concourse.bass_utils import run_bass_kernel_spmd as _run

    consts = {
        "ident": _np.eye(P, dtype=_np.float32),
        "rope_local": _rope_table(0, HEAD),
        "rope_q": _rope_table(TOK, XHEAD),
        "rope_mem": _rope_table(0, XHEAD),
        "masks": _mask_table(),
    }
    nc = _bacc.Bacc("TRN2", target_bir_lowering=False, num_devices=1)
    arrays, args = {}, []
    for name, a in [(n, inputs[n]) for n in _INS] + list(consts.items()):
        a = _np.ascontiguousarray(a)
        arrays[f"in_{name}_dram"] = a
        args.append(nc.dram_tensor(f"in_{name}_dram", a.shape, mybir.dt.from_np(a.dtype), kind="ExternalInput").ap())
    args.append(nc.dram_tensor("out_0_dram", (1, TOK, D), F32, kind="ExternalOutput").ap())
    hybrid_layer(nc, *args)
    r = _run(nc, [arrays], core_ids=[0])
    return r.results[0]["out_0_dram"]
```
